# Optimizing a Trainium2 kernel written in Bass

```python
import math
import jax, jax.numpy as jnp
from jax import lax
import numpy as np

D_MODEL = 1024
BATCH = 1
SEQ = 512
DEPTH = 1

ATTN_HEADS = 8
ATTN_KV_HEADS = 2
HEAD_DIM = 64
ATTN_WIDTH = ATTN_HEADS * HEAD_DIM
WINDOW = 128
ATTN_BLOCK = 128
N_BUCKETS = 32
MAX_DISTANCE = 128
SSD_HEADS = 8
SSD_HEAD_DIM = 64
SSD_INNER = SSD_HEADS * SSD_HEAD_DIM
SSD_STATE = 128
SSD_GROUPS = 2
SSD_CONV = 4
SSD_CHUNK = 128
MIX_WIDTH = ATTN_WIDTH + SSD_INNER
PEER_HEADS = 8
N_KEYS = 128
N_EXPERTS = N_KEYS * N_KEYS
PEER_KEY_DIM = 256
PEER_HALF = PEER_KEY_DIM // 2
PEER_TOPK = 16
PEER_BLOCK = 128
EPS = 1e-6

KV_COLS = ATTN_KV_HEADS * HEAD_DIM
XBC_COLS = SSD_INNER + 2 * SSD_GROUPS * SSD_STATE
OFF_K = ATTN_WIDTH
OFF_V = OFF_K + KV_COLS
OFF_Z = OFF_V + KV_COLS
OFF_XBC = OFF_Z + SSD_INNER
OFF_DT = OFF_XBC + XBC_COLS
IN_COLS = OFF_DT + SSD_HEADS

kernel_name = 'hymba_swa_ssd_peer_block'

def rms_norm(x, w):
    xf = x.astype(jnp.float32)
    y = xf * lax.rsqrt(jnp.mean(xf * xf, axis=-1, keepdims=True) + EPS)
    return (y * w.astype(jnp.float32)).astype(x.dtype)

def t5_bucket(dist):
    n = jnp.maximum(dist, 0)
    max_exact = N_BUCKETS // 2
    nf = jnp.maximum(n, 1).astype(jnp.float32)
    large = max_exact + (jnp.log(nf / max_exact) / math.log(MAX_DISTANCE / max_exact)
                         * (N_BUCKETS - max_exact)).astype(jnp.int32)
    large = jnp.minimum(large, N_BUCKETS - 1)
    return jnp.where(n < max_exact, n, large)

def sliding_window_attention(q, k, v, sinks, rel_bias):
    b, s = q.shape[0], q.shape[1]
    nb = s // ATTN_BLOCK
    grp = ATTN_HEADS // ATTN_KV_HEADS
    qb = q.reshape(b, nb, ATTN_BLOCK, ATTN_KV_HEADS, grp, HEAD_DIM)

    def band(t):
        tp = jnp.pad(t, ((0, 0), (ATTN_BLOCK, 0), (0, 0), (0, 0)))
        tp = tp.reshape(b, nb + 1, ATTN_BLOCK, ATTN_KV_HEADS, HEAD_DIM)
        return jnp.concatenate([tp[:, :-1], tp[:, 1:]], axis=2)

    kb, vb = band(k), band(v)
    scores = jnp.einsum('bnqhgd,bnkhd->bnhgqk', qb, kb).astype(jnp.float32) * (HEAD_DIM ** -0.5)
    qi = jnp.arange(ATTN_BLOCK)[:, None]
    kj = jnp.arange(2 * ATTN_BLOCK)[None, :]
    dist = qi + ATTN_BLOCK - kj
    in_window = (dist >= 0) & (dist < WINDOW)
    key_pos = jnp.arange(nb)[:, None, None] * ATTN_BLOCK - ATTN_BLOCK + kj[None]
    valid = in_window[None] & (key_pos >= 0)
    bias = rel_bias[t5_bucket(dist)].astype(jnp.float32)
    bias = bias.transpose(2, 0, 1).reshape(ATTN_KV_HEADS, grp, ATTN_BLOCK, 2 * ATTN_BLOCK)
    scores = jnp.where(valid[None, :, None, None], scores + bias, -jnp.inf)
    sink = sinks.astype(jnp.float32).reshape(ATTN_KV_HEADS, grp)[:, :, None, None]
    m = jnp.maximum(jnp.max(scores, axis=-1, keepdims=True), sink)
    p = jnp.exp(scores - m)
    denom = jnp.sum(p, axis=-1, keepdims=True) + jnp.exp(sink - m)
    probs = (p / denom).astype(v.dtype)
    out = jnp.einsum('bnhgqk,bnkhd->bnqhgd', probs, vb)
    return out.reshape(b, s, ATTN_WIDTH)

def causal_depthwise_conv(x, w, bias):
    kw = w.shape[0]
    y = lax.conv_general_dilated(x, w[:, None, :], window_strides=(1,), padding=[(kw - 1, 0)],
                                 dimension_numbers=('NWC', 'WIO', 'NWC'),
                                 feature_group_count=x.shape[-1])
    return y + bias

def ssd_scan(x, dt, A, Bm, Cm):
    f32 = jnp.float32
    b, s, h, p = x.shape
    c = s // SSD_CHUNK
    L = SSD_CHUNK
    g = SSD_GROUPS
    r = h // g
    X = (x.astype(f32) * dt[..., None]).reshape(b, c, L, g, r, p)
    a = (dt * A).reshape(b, c, L, g, r).transpose(0, 3, 4, 1, 2)
    a_cum = jnp.cumsum(a, axis=-1)
    Bg = Bm.astype(f32).reshape(b, c, L, g, -1)
    Cg = Cm.astype(f32).reshape(b, c, L, g, -1)
    seg = a_cum[..., :, None] - a_cum[..., None, :]
    causal = jnp.tril(jnp.ones((L, L), dtype=bool))
    Lmat = jnp.where(causal, jnp.exp(jnp.where(causal, seg, 0.0)), 0.0)
    CB = jnp.einsum('bclgn,bcsgn->bgcls', Cg, Bg)
    y_diag = jnp.einsum('bgrcls,bcsgrp->bclgrp', CB[:, :, None] * Lmat, X)
    decay_to_end = jnp.exp(a_cum[..., -1:] - a_cum).transpose(0, 3, 4, 1, 2)
    states = jnp.einsum('bclgn,bclgrp->bcgrpn', Bg, X * decay_to_end[..., None])
    chunk_decay = jnp.exp(a_cum[..., -1]).transpose(3, 0, 1, 2)

    def step(h_prev, inp):
        st, dec = inp
        return h_prev * dec[..., None, None] + st, h_prev

    h0 = jnp.zeros((b, g, r, p, Bg.shape[-1]), f32)
    _, prev_states = lax.scan(step, h0, (states.transpose(1, 0, 2, 3, 4, 5), chunk_decay))
    decay_from_start = jnp.exp(a_cum).transpose(0, 3, 4, 1, 2)
    y_off = jnp.einsum('bclgn,cbgrpn->bclgrp', Cg, prev_states) * decay_from_start[..., None]
    return (y_diag + y_off).reshape(b, s, h, p)

def hybrid_mixer(xn, w_in, conv_w, conv_b, dt_bias, a_log, d_skip, ssd_norm_w, sinks, w_out, rel_bias):
    b, s, _ = xn.shape
    proj = xn @ w_in
    q = proj[..., :OFF_K].reshape(b, s, ATTN_HEADS, HEAD_DIM)
    k = proj[..., OFF_K:OFF_V].reshape(b, s, ATTN_KV_HEADS, HEAD_DIM)
    v = proj[..., OFF_V:OFF_Z].reshape(b, s, ATTN_KV_HEADS, HEAD_DIM)
    z = proj[..., OFF_Z:OFF_XBC]
    xbc = proj[..., OFF_XBC:OFF_DT]
    dt_raw = proj[..., OFF_DT:]
    attn_out = sliding_window_attention(q, k, v, sinks, rel_bias)
    xbc = jax.nn.silu(causal_depthwise_conv(xbc, conv_w, conv_b))
    xs = xbc[..., :SSD_INNER].reshape(b, s, SSD_HEADS, SSD_HEAD_DIM)
    Bm = xbc[..., SSD_INNER:SSD_INNER + SSD_GROUPS * SSD_STATE].reshape(b, s, SSD_GROUPS, SSD_STATE)
    Cm = xbc[..., SSD_INNER + SSD_GROUPS * SSD_STATE:].reshape(b, s, SSD_GROUPS, SSD_STATE)
    dt = jax.nn.softplus(dt_raw.astype(jnp.float32) + dt_bias.astype(jnp.float32))
    A = -jnp.exp(a_log.astype(jnp.float32))
    y = ssd_scan(xs, dt, A, Bm, Cm) + d_skip.astype(jnp.float32)[:, None] * xs.astype(jnp.float32)
    y = y.reshape(b, s, SSD_INNER) * jax.nn.silu(z.astype(jnp.float32))
    ssd_out = rms_norm(y, ssd_norm_w).astype(xn.dtype)
    return jnp.concatenate([attn_out, ssd_out], axis=-1) @ w_out

def peer(xn, w_query, sub_keys1, sub_keys2, expert_down, expert_up):
    f32 = jnp.float32
    b, s, d = xn.shape
    q = (xn @ w_query).reshape(b, s, PEER_HEADS, 2, PEER_HALF).astype(f32)
    s1 = jnp.einsum('bshk,nk->bshn', q[..., 0, :], sub_keys1.astype(f32))
    s2 = jnp.einsum('bshk,nk->bshn', q[..., 1, :], sub_keys2.astype(f32))
    v1, i1 = lax.top_k(s1, PEER_TOPK)
    v2, i2 = lax.top_k(s2, PEER_TOPK)
    cand = (v1[..., :, None] + v2[..., None, :]).reshape(b, s, PEER_HEADS, PEER_TOPK * PEER_TOPK)
    cand_idx = (i1[..., :, None] * N_KEYS + i2[..., None, :]).reshape(b, s, PEER_HEADS, PEER_TOPK * PEER_TOPK)
    top_s, pos = lax.top_k(cand, PEER_TOPK)
    idx = jnp.take_along_axis(cand_idx, pos, axis=-1)
    gates = jax.nn.softmax(top_s, axis=-1)
    nblk = s // PEER_BLOCK

    def to_blocks(t):
        return t.reshape((b, nblk, PEER_BLOCK) + t.shape[2:]).swapaxes(0, 1)

    def eval_block(args):
        xb, ib, gb = args
        u = expert_down[ib]
        pre = jnp.einsum('bthkd,btd->bthk', u, xb).astype(f32)
        act = (jax.nn.gelu(pre, approximate=False) * gb).astype(xb.dtype)
        return jnp.einsum('bthk,bthkd->btd', act, expert_up[ib])

    out = lax.map(eval_block, (to_blocks(xn), to_blocks(idx), to_blocks(gates)))
    return out.swapaxes(0, 1).reshape(b, s, d)

def setup_inputs(seed: int = 0) -> dict:
    key = jax.random.key(seed)
    ks = jax.random.split(key, 20)
    f32 = jnp.float32
    nrm = lambda k, shape, scale: (jax.random.normal(k, shape, f32) * scale)
    dt0 = jnp.exp(jax.random.uniform(ks[5], (DEPTH, SSD_HEADS), f32)
                  * (math.log(0.1) - math.log(0.001)) + math.log(0.001))
    return {
        'x': nrm(ks[0], (BATCH, SEQ, D_MODEL), 1.0),
        'norm_mix': 1.0 + nrm(ks[1], (DEPTH, D_MODEL), 0.05),
        'w_in': nrm(ks[2], (DEPTH, D_MODEL, IN_COLS), D_MODEL ** -0.5),
        'conv_w': nrm(ks[3], (DEPTH, SSD_CONV, XBC_COLS), SSD_CONV ** -0.5),
        'conv_b': nrm(ks[4], (DEPTH, XBC_COLS), 0.02),
        'dt_bias': dt0 + jnp.log(-jnp.expm1(-dt0)),
        'a_log': jnp.log(jax.random.uniform(ks[6], (DEPTH, SSD_HEADS), f32, 1.0, 16.0)),
        'd_skip': 1.0 + nrm(ks[7], (DEPTH, SSD_HEADS), 0.1),
        'ssd_norm_w': 1.0 + nrm(ks[8], (DEPTH, SSD_INNER), 0.05),
        'attn_sinks': nrm(ks[9], (DEPTH, ATTN_HEADS), 1.0),
        'w_out': nrm(ks[10], (DEPTH, MIX_WIDTH, D_MODEL), MIX_WIDTH ** -0.5),
        'rel_bias': nrm(ks[11], (N_BUCKETS, ATTN_HEADS), 0.5),
        'norm_ffn': 1.0 + nrm(ks[12], (DEPTH, D_MODEL), 0.05),
        'w_query': nrm(ks[13], (DEPTH, D_MODEL, PEER_HEADS * PEER_KEY_DIM), D_MODEL ** -0.5),
        'sub_keys1': nrm(ks[14], (DEPTH, N_KEYS, PEER_HALF), PEER_HALF ** -0.5),
        'sub_keys2': nrm(ks[15], (DEPTH, N_KEYS, PEER_HALF), PEER_HALF ** -0.5),
        'expert_down': nrm(ks[16], (DEPTH, N_EXPERTS, D_MODEL), D_MODEL ** -0.5),
        'expert_up': nrm(ks[17], (DEPTH, N_EXPERTS, D_MODEL), PEER_HEADS ** -0.5),
        'norm_final': 1.0 + nrm(ks[18], (D_MODEL,), 0.05),
    }

def reference(x, norm_mix, w_in, conv_w, conv_b, dt_bias, a_log, d_skip, ssd_norm_w, attn_sinks,
              w_out, rel_bias, norm_ffn, w_query, sub_keys1, sub_keys2, expert_down, expert_up,
              norm_final):
    h = x
    for l in range(DEPTH):
        h = h + hybrid_mixer(rms_norm(h, norm_mix[l]), w_in[l], conv_w[l], conv_b[l], dt_bias[l],
                             a_log[l], d_skip[l], ssd_norm_w[l], attn_sinks[l], w_out[l], rel_bias)
        h = h + peer(rms_norm(h, norm_ffn[l]), w_query[l], sub_keys1[l], sub_keys2[l],
                     expert_down[l], expert_up[l])
    return rms_norm(h, norm_final)


_drawn_inputs = setup_inputs


def setup_inputs(seed=0):
    import zlib

    import numpy as np

    out = dict(_drawn_inputs(seed))
    spreads = {}
    factors = {'attn_sinks': 3.907}
    for name, (base, spread) in spreads.items():
        noise = np.random.default_rng([zlib.crc32(name.encode()), seed]).standard_normal(out[name].shape)
        drawn = base * np.exp(spread * noise) if base else spread * noise
        out[name] = __import__('jax').numpy.asarray(drawn.astype(out[name].dtype))
    for name, factor in factors.items():
        out[name] = (out[name] * factor).astype(out[name].dtype)
    return out
```

```python
import math
from contextlib import ExitStack

import numpy as np

import concourse.bass as bass
from concourse import mybir

ALU = mybir.AluOpType
ACT = mybir.ActivationFunctionType
AX = mybir.AxisListType
F32 = mybir.dt.float32
I32 = mybir.dt.int32
U32 = mybir.dt.uint32

P = 128
D = 1024
KT = D // P
SEQ = 512
NT = SEQ // P
HEADS, KV_HEADS, HD = 8, 2, 64
WINDOW = 128
N_BUCKETS, MAX_DISTANCE = 32, 128
SH, SP, SN, SG = 8, 64, 128, 2
SR = SH // SG
CONV = 4
XBC = SH * SP + 2 * SG * SN
NXB = XBC // P
PH, NK, TOPK = 8, 128, 16
SLOTS = PH * TOPK
GROUP = 8
EPS = 1e-6
NEG = -1e30
LOWEST = -3.0e38
LW = 3 * P
NBLK = NXB + 5 + 1 + 4
RING = 5
B_K, B_Q, B_V, B_Z = NXB, NXB + 1, NXB + 5, NXB + 6


def layer(nc, x, w_in_blocks, w_dt, norm_mix, conv_w, conv_b, dt_bias, a_log, d_skip, ssd_norm_w, sinks, w_out,
          rel_bias, bucket_line, norm_ffn, w_query, keys1_t, keys2_t, expert_down, expert_up, norm_final, out):
    line_dram = nc.dram_tensor("line_scratch", (P, HEADS * LW), F32, kind="Internal").ap()
    with ExitStack() as ctx:
        def sb(name, shape, dt=F32):
            return ctx.enter_context(nc.sbuf_tensor(name, shape, dt))

        SEMS = {}

        def sem(name):
            if name not in SEMS:
                SEMS[name] = ctx.enter_context(nc.semaphore(name))
            return SEMS[name]

        arena = sb("arena", [P, 24 * D])
        arena2 = sb("arena2", [P, 6 * D])
        wq = sb("wq", [P, KT, PH * 2 * P])
        h = sb("h", [P, NT, D])

        def slot(i, n=1, of=arena):
            return of[:, i * D:(i + n) * D]

        xnT = slot(0, 4).rearrange("p (k t) -> p k t", k=KT)
        ring = slot(4, RING).rearrange("p (s k c) -> p s k c", s=RING, k=KT)
        PAD = CONV - 1
        xraw = arena[:, 9 * D:9 * D + NXB * (SEQ + PAD)].rearrange("p (j t) -> p j t", j=NXB)
        xconv = slot(14, 4).rearrange("p (j t) -> p j t", j=NXB)
        zs = slot(18, 2).rearrange("p (t c) -> p t c", t=NT)
        qkT = arena[:, 20 * D:20 * D + 5 * SEQ].rearrange("p (j t) -> p j t", j=5)
        v_sb = arena[:, 23 * D:23 * D + NT * P].rearrange("p (t c) -> p t c", t=NT)
        wo = slot(0, 8).rearrange("p (k c) -> p k c", k=KT)
        bias = slot(0, 2, arena2).rearrange("p (h k) -> p h k", h=HEADS)
        prob = slot(2, 2, arena2).rearrange("p (h k) -> p h k", h=HEADS)
        probT = slot(4, 2, arena2).rearrange("p (b c) -> p b c", b=4)
        xn = slot(4, 2, arena2).rearrange("p (b c) -> p b c", b=2)
        line = arena[:, 14 * D:14 * D + HEADS * LW].rearrange("p (h m) -> p h m", h=HEADS)
        buckets = arena[0:N_BUCKETS + 1, 18 * D:18 * D + LW]
        xs = slot(9)[:, 0:512]
        xdt = slot(9)[:, 512:1024]
        xend = slot(10)[:, 0:512]
        bnat = slot(10)[:, 512:768]
        cbT = slot(10)[:, 768:1024]
        decay = slot(11).rearrange("p (g c) -> p g c", g=SG)
        mix = slot(12)
        mixT = slot(13).rearrange("p (k t) -> p k t", k=KT)
        y1 = arena[:, 23 * D + 512:24 * D]
        y2 = arena[:, 22 * D + 512:23 * D]
        down = slot(0, 8).rearrange("p (s c) -> p s c", s=8)
        up = slot(8, 8).rearrange("p (s c) -> p s c", s=8)
        xn2 = slot(16, 2).rearrange("p (b c) -> p b c", b=2)
        xn2T = slot(18).rearrange("p (k t) -> p k t", k=KT)
        qT = slot(19, 2).rearrange("p (j t) -> p j t", j=2 * PH)
        cand = slot(19, 2).rearrange("p (h c) -> p h c", h=PH)
        score = slot(21, 2).rearrange("p (j n) -> p j n", j=2 * PH)
        hit = slot(0, 2, arena2)
        hit4 = hit.rearrange("p (h k a) -> p h k a", h=PH, k=TOPK)
        diag = slot(2, 1, arena2).rearrange("p (s c) -> p s c", s=GROUP)
        w_ffn = slot(3, 1, arena2)
        w_fin = slot(4, 1, arena2)
        keep = slot(5, 1, arena2)
        idx = keep[:, 0:256].bitcast(I32).rearrange("p (b m) -> p b m", b=2)
        gate = keep[:, 256:512].rearrange("p (b m) -> p b m", b=2)
        keysT = keep[:, 512:768].rearrange("p (s n) -> p s n", s=2)

        ident = sb("ident", [P, P])
        tri = sb("tri", [P, P])
        negm = sb("negm", [P, P])
        ones = sb("ones", [P, P])
        state = sb("state", [P, 512])
        wn = sb("wn", [P, 512])
        wmix = sb("wmix", [P, KT])
        early = slot(2, 1, arena2)
        w_dt_sb = early[:, 0:64].rearrange("p (k c) -> p k c", k=KT)
        cw = early[:, 64:96].rearrange("p (w j) -> p w j", w=CONV)
        cb = early[:, 96:104]
        rb = sb("rb", [N_BUCKETS + 1, HEADS])
        hrow = sb("hrow", [P, 4, SH])
        ss = sb("ss", [P, 16])
        dtv = sb("dtv", [P, 8, NT * SH])
        sm = sb("sm", [P, 12, SH])
        last = slot(23)
        val = last[:, 0:256].rearrange("p (j k) -> p j k", k=TOPK)
        vidf = last[:, 256:512].rearrange("p (j k) -> p j k", k=TOPK)
        vidx = last[:, 512:768].bitcast(U32).rearrange("p (j k) -> p j k", k=TOPK)
        top = last[:, 768:896].rearrange("p (j k) -> p j k", k=TOPK)
        tpos = last[:, 896:1024].bitcast(U32).rearrange("p (j k) -> p j k", k=TOPK)
        tabf = state[:].rearrange("p (i m) -> p i m", i=4)
        tab = wn[:, 0:2 * SLOTS].bitcast(U32).rearrange("p (i m) -> p i m", i=2)
        iota16 = keep[:, 856:872]
        iota16i = sb("iota16i", [P, TOPK], I32)
        gsum = keep[:, 832:856].rearrange("p (i h) -> p i h", i=3)
        inow = keep[:, 768:784].bitcast(I32).rearrange("p (b i) -> p b i", b=2)
        gnow, pre, gel = (keep[:, 784 + 16 * i:800 + 16 * i].rearrange("p (b i) -> p b i", b=2) for i in range(3))
        sq = sb("sq", [P, 2])
        actv = sb("actv", [P, 2, GROUP])

        ps = [ctx.enter_context(nc.psum_tensor(f"ps{i}", [P, 512], F32)) for i in range(8)]

        block = ctx.enter_context(nc.Block())

        def link(eng, ins, name, count):
            count[name] = count.get(name, 0) + 1
            ins.then_inc(sem(name), 1)
            eng.wait_ge(sem(name), count[name])

        LOADS = {}

        @block.sync
        def _(sp):
            for t in range(NT):
                sp.dma_start(h[:, t, :], x[0, t * P:(t + 1) * P, :]).then_inc(sem(f"x_in{t}"), 16)
                if t == 0:
                    sp.dma_start(buckets, bucket_line).then_inc(sem("line_in"), 16)
                    sp.dma_start(rb[0:N_BUCKETS, :], rel_bias).then_inc(sem("line_in"), 16)
                    sp.dma_start(wmix[:], norm_mix).then_inc(sem("wmix_in"), 16)
            for b in range(NBLK):
                if b >= RING:
                    sp.wait_ge(sem("block_used"), b - RING + 1)
                sp.dma_start(ring[:, b % RING], w_in_blocks[b].rearrange("p (k c) -> p k c", k=KT)
                             ).then_inc(sem(f"ring{b % RING}"), 16)
                if b == 2:
                    sp.dma_start(cw, conv_w).then_inc(sem("conv_in"), 16)
                    sp.dma_start(cb, conv_b).then_inc(sem("conv_in"), 16)
                if b == 4:
                    sp.dma_start(w_dt_sb, w_dt.rearrange("p (k c) -> p k c", k=KT)).then_inc(sem("wdt_in"), 16)
                    for i, row in enumerate((dt_bias, a_log, d_skip, sinks)):
                        sp.dma_start(hrow[:, i, :], row.to_broadcast([P, SH])).then_inc(sem("rows_in"), 16)
                    sp.dma_start(wn[:], ssd_norm_w.to_broadcast([P, 512])).then_inc(sem("rows_in"), 16)
                    sp.wait_ge(sem("line_done"), HEADS)
                    sp.dma_start(line_dram, line).then_inc(sem("line_out"), 16)
                    sp.wait_ge(sem("line_out"), 16)
                    skew = bass.AP(line_dram.tensor, P - 1, [[HEADS * LW - 1, P], [LW, HEADS], [1, 2 * P]])
                    sp.dma_start(bias, skew).then_inc(sem("bias_in"), 16)
            sp.wait_ge(sem("block_used"), NBLK + 1)
            sp.dma_start(wo, w_out.rearrange("(k p) c -> p k c", p=P)).then_inc(sem("wo_in"), 16)
            sp.dma_start(wq[:], w_query.rearrange("(k p) c -> p k c", p=P)).then_inc(sem("wq_in"), 16)
            sp.wait_ge(sem("h_mixed"), NT)
            sp.dma_start(keysT[:, 0, :], keys1_t).then_inc(sem("wq_in"), 16)
            sp.dma_start(keysT[:, 1, :], keys2_t).then_inc(sem("wq_in"), 16)
            sp.dma_start(w_ffn, norm_ffn.to_broadcast([P, D])).then_inc(sem("wffn_in"), 16)
            sp.dma_start(w_fin, norm_final.to_broadcast([P, D])).then_inc(sem("wffn_in"), 16)
            for t in range(NT):
                sp.wait_ge(sem("final_ready"), t + 1)
                sp.dma_start(out[0, t * P:(t + 1) * P, :], xn2[:, t % 2, :]).then_inc(sem(f"stored{t}"), 16)
            for t in range(NT):
                sp.wait_ge(sem(f"stored{t}"), 16)

        @block.gpsimd
        def _(gp):
            n = {}
            link(gp, gp.memset(ones[:], 1.0), "const", n)
            link(gp, gp.memset(negm[:], 0.0), "const", n)
            link(gp, gp.affine_select(out=ident[:], in_=ones[:], compare_op=ALU.is_equal, fill=0.0, base=0,
                                      pattern=[[-1, P]], channel_multiplier=1), "const", n)
            link(gp, gp.affine_select(out=tri[:], in_=ones[:], compare_op=ALU.is_ge, fill=0.0, base=0,
                                      pattern=[[1, P]], channel_multiplier=-1), "const", n)
            link(gp, gp.affine_select(out=negm[:], in_=negm[:], compare_op=ALU.is_ge, fill=NEG, base=0,
                                      pattern=[[1, P]], channel_multiplier=-1), "const", n)
            link(gp, gp.iota(iota16i[:], pattern=[[1, TOPK]], base=0, channel_multiplier=0), "const", n)
            for j in range(NXB):
                link(gp, gp.memset(xraw[:, j, 0:PAD], 0.0), "const", n)
            LOADS["const"] = n["const"]
            for t in range(NT):
                gp.wait_ge(sem("routed"), t + 1)
                with gp.Fori(0, SLOTS // GROUP // 2) as r:
                    for half in range(2):
                        g0 = t * (SLOTS // GROUP) + half
                        if half == 0:
                            gp.wait_ge(sem("up_free"), 8 * (g0 + 2 * r) + 8)
                        gp.tensor_copy(inow[:, half], idx[:, t % 2, bass.ds((2 * r + half) * GROUP, GROUP)]
                                       ).then_inc(sem("inow_ready"), 1)
                        gp.tensor_copy(gnow[:, half], gate[:, t % 2, bass.ds((2 * r + half) * GROUP, GROUP)]
                                       ).then_inc(sem("gnow_ready"), 1)
                        gp.wait_ge(sem("inow_ready"), g0 + 2 * r + 1)
                        for i in range(GROUP):
                            gp.wait_ge(sem("dots"), 8 * (g0 + 2 * r) + i + 1)
                            gp.nop(nofuse=True)
                            gp.indirect_dma_start(down[:, i, :], None, expert_down,
                                                  bass.IndirectOffsetOnAxis(ap=inow[:, half, i:i + 1], axis=0)
                                                  ).then_inc(sem(f"down{i}"), 16)
                        for i in range(GROUP):
                            gp.wait_ge(sem("up_free"), 8 * (g0 + 2 * r) + i + 1)
                            gp.nop(nofuse=True)
                            gp.indirect_dma_start(up[:, i, :], None, expert_up,
                                                  bass.IndirectOffsetOnAxis(ap=inow[:, half, i:i + 1], axis=0)
                                                  ).then_inc(sem(f"up{i}"), 16)

        @block.scalar
        def _(act):
            n = {}

            def copy(o, i, name="act_step", func=ACT.Copy, **kw):
                link(act, nc.scalar.activation(o, i, func, **kw), name, n)

            for t in range(NT):
                act.wait_ge(sem(f"x_in{t}"), 16)
                if t:
                    act.wait_ge(sem("xn_ready"), t)
                copy(slot(19), h[:, t, :], "sq_x", ACT.Square, accum_out=ss[:, t:t + 1])
            for hh in range(HEADS):
                act.wait_ge(sem("line_ps"), hh + 1)
                copy(line[:, hh, :], ps[4 + hh % 2][:, 0:LW], "line_done")
            for b in range(NBLK + 1):
                act.wait_ge(sem("block_used"), b + 1)
                src = ps[b % 4]
                if b < NXB:
                    copy(xraw[:, b, PAD:], src[:], "proj_out")
                elif b < B_V:
                    copy(qkT[:, b - B_K, :], src[:], "proj_out")
                elif b == B_V:
                    copy(v_sb, src[:].rearrange("p (t c) -> p t c", t=NT), "proj_out")
                elif b < NBLK:
                    copy(zs[:, :, (b - B_Z) * P:(b - B_Z + 1) * P], src[:].rearrange("p (t c) -> p t c", t=NT),
                         "proj_out", ACT.Silu)
                else:
                    copy(dtv[:, 0, :], src[:, 0:NT * SH], "proj_out")
            act.wait_ge(sem("conv_in"), 32)
            for j in range(NXB):
                act.wait_ge(sem("conv_done"), j + 1)
                copy(xconv[:, j, :], xconv[:, j, :], "conv_act", ACT.Silu, bias=cb[:, j:j + 1])
            act.wait_ge(sem("dt_abs"), 1)
            copy(dtv[:, 2, :], dtv[:, 1, :], "dt_exp", ACT.Exp, scale=-1.0)
            copy(hrow[:, 1, :], hrow[:, 1, :], "dt_exp", ACT.Exp)

            for c in range(NT):
                act.wait_ge(sem("acum_ps"), c + 1)
                if c:
                    act.wait_ge(sem("y_done"), c)
                copy(sm[:, 0, :], ps[7][:, 0:8], "acum_sb")
                copy(sm[:, 1, :], ps[7][:, 0:8], "decays", ACT.Exp)
                copy(sm[:, 2, :], ps[7][:, 8:16], "decays", ACT.Exp)
                act.wait_ge(sem("to_end"), c + 1)
                copy(sm[:, 3, :], sm[:, 4, :], "decays", ACT.Exp)
                act.wait_ge(sem("nat_ps"), c + 1)
                copy(xs, ps[0][:], "nat_sb")
                copy(bnat, ps[1][:, 0:256], "nat_sb")
                copy(cbT, ps[1][:, 256:512], "nat_sb")
                for g in range(SG):
                    act.wait_ge(sem("seg_sb"), SG * c + g + 1)
                    copy(decay[:, g], decay[:, g], "seg_exp", ACT.Exp)
                act.wait_ge(sem("neg_max"), c + 1)
                if c:
                    act.wait_ge(sem("pt_ps"), c)
                k0 = 0 if c else P
                for hh in range(HEADS):
                    copy(prob[:, hh, k0:], prob[:, hh, k0:], "prob_exp", ACT.Exp, bias=sm[:, 6, hh:hh + 1],
                         accum_out=sm[:, 8, hh:hh + 1])
                copy(sm[:, 9, :], sm[:, 7, :], "prob_exp", ACT.Exp)
                for b in range(4):
                    if c:
                        act.wait_ge(sem("pt_ps"), c + 1)
                        copy(probT[:, b, :], ps[4 + b][:], "pt_sb")
                    else:
                        act.wait_ge(sem("pt_ps"), c + 1)
                        half = ps[4 + b][:].rearrange("p (i q) -> p i q", i=4)[:, 1::2, :]
                        copy(probT[:, b, :].rearrange("p (i q) -> p i q", i=4)[:, 1::2, :], half, "pt_sb")
                act.wait_ge(sem("mixT_ps"), c + 1)
                for b in range(2):
                    copy(mixT[:, 4 * b:4 * b + 4, :], ps[1 + b][:].rearrange("p (k t) -> p k t", k=4), "mixT_sb")

            def route(t):
                if t == 0:
                    act.wait_ge(sem("h_mixed"), NT)
                else:
                    act.wait_ge(sem("route_mid"), t)
                copy(hit[:, 0:D], h[:, t, :], "sq_h", ACT.Square, accum_out=ss[:, 4 + t:5 + t])
                act.wait_ge(sem("xn2T_ps"), t + 1)
                for b in range(2):
                    copy(xn2T[:, 4 * b:4 * b + 4, :], ps[b][:].rearrange("p (k t) -> p k t", k=4), "xn2T_sb")
                for b in range(4):
                    act.wait_ge(sem("q_ps"), 4 * t + b + 1)
                    copy(qT[:, 4 * b:4 * b + 4, :], ps[2 + b % 2][:].rearrange("p (j t) -> p j t", j=4), "q_sb")
                for b in range(4):
                    act.wait_ge(sem("s_ps"), 4 * t + b + 1)
                    copy(score[:, 4 * b:4 * b + 4, :], ps[b % 2][:].rearrange("p (j t) -> p j t", j=4), "s_sb")
                act.wait_ge(sem("gate_in"), t + 1)
                copy(tabf[:, 3, :], tabf[:, 2, :], "gate_exp", ACT.Exp)

            def experts(t):
                with act.Fori(0, SLOTS // GROUP // 2) as r:
                    for half in range(2):
                        g0 = t * (SLOTS // GROUP) + half
                        act.wait_ge(sem("dots"), 8 * (g0 + 2 * r) + 16)
                        nc.scalar.activation(gel[:, half], pre[:, half], ACT.Gelu).then_inc(sem("gelu"), 1)
                        act.wait_ge(sem("act_ready"), g0 + 2 * r + 1)
                        for i in range(GROUP):
                            act.wait_ge(sem("up_free"), 8 * (g0 + 2 * r) + i + 1)
                            nc.scalar.activation(diag[:, i, :], ident[:], ACT.Copy, scale=actv[:, half, i:i + 1]
                                                 ).then_inc(sem("diag"), 1)
                act.wait_ge(sem("peer_done"), t + 1)
                final = xn2[:, t % 2, :]
                copy(final[:, 0:512], ps[6][:], "fin_sq", ACT.Square, accum_out=ss[:, 12:13])
                copy(final[:, 512:], ps[7][:], "fin_sq", ACT.Square, accum_out=ss[:, 13:14])

            for t in range(NT):
                route(t)
                experts(t)

        @block.vector
        def _(dve):
            n = {}
            v = nc.vector

            def go(ins, name="dve_step"):
                link(dve, ins, name, n)

            def rms(o, i, width, name):
                m, t = sq[:, 0:1], sq[:, 1:2]
                go(v.tensor_scalar(m, i, 1.0 / width, EPS, ALU.mult, ALU.add))
                go(v.tensor_scalar(t.bitcast(I32), m.bitcast(I32), 1, None, ALU.logical_shift_right))
                go(v.tensor_scalar(o.bitcast(I32), t.bitcast(I32), -1.0, float(0x5f3759df), ALU.mult, ALU.add))
                for step in range(3):
                    go(v.scalar_tensor_tensor(t, o, m, o, ALU.mult, ALU.mult))
                    go(v.tensor_scalar(t, t, -0.5, 1.5, ALU.mult, ALU.add))
                    go(v.tensor_tensor(o, o, t, ALU.mult), name if step == 2 else "dve_step")

            v.memset(actv[:, 0], 0.0).then_inc(sem("dots"), 8)
            v.memset(actv[:, 1], 0.0).then_inc(sem("up_free"), 8)
            go(v.memset(rb[N_BUCKETS:N_BUCKETS + 1, :], 1.0), "rb_ones")
            for t in range(NT):
                dve.wait_ge(sem("sq_x"), t + 1)
                rms(ss[:, 8 + t:9 + t], ss[:, t:t + 1], D, "dve_step")
                if t >= 2:
                    dve.wait_ge(sem("xT_ps"), t - 1)
                go(v.tensor_scalar(xn[:, t % 2, :], h[:, t, :], ss[:, 8 + t:9 + t], None, ALU.mult), "xn_ready")
                dve.wait_ge(sem("xT_ps"), t + 1)
                dve.wait_ge(sem("wmix_in"), 16)
                for b in range(2):
                    go(v.tensor_tensor(xnT[:, 4 * b:4 * b + 4, t * P:(t + 1) * P],
                                       ps[2 * (t % 2) + b][:].rearrange("p (k t) -> p k t", k=4),
                                       wmix[:, 4 * b:4 * b + 4].unsqueeze(2).to_broadcast([P, 4, P]), ALU.mult), "xT_sb")
            dve.wait_ge(sem("conv_in"), 32)
            dve.wait_ge(sem("const"), LOADS["const"])
            dve.wait_ge(sem("line_out"), 16)
            for j in range(NXB):
                dve.wait_ge(sem("proj_out"), j + 1)
                go(v.tensor_scalar(xconv[:, j, :], xraw[:, j, 0:SEQ], cw[:, 0, j:j + 1], None, ALU.mult))
                for k in range(1, CONV):
                    go(v.scalar_tensor_tensor(xconv[:, j, :], xraw[:, j, k:k + SEQ], cw[:, k, j:j + 1], xconv[:, j, :],
                                              ALU.mult, ALU.add), "conv_done" if k == CONV - 1 else "dve_step")
            dve.wait_ge(sem("rows_in"), 80)
            dve.wait_ge(sem("proj_out"), NBLK + 1)
            u, ab, ex, s, s2, acc, dt, a = (dtv[:, i, :] for i in range(8))
            br = lambda i: hrow[:, i, :].unsqueeze(1).to_broadcast([P, NT, SH])
            as4 = lambda z: z.rearrange("p (t h) -> p t h", t=NT)
            go(v.tensor_tensor(as4(u), as4(u), br(0), ALU.add))
            go(v.tensor_scalar(s, u, -1.0, None, ALU.mult))
            go(v.tensor_tensor(ab, u, s, ALU.max), "dt_abs")
            dve.wait_ge(sem("dt_exp"), 2)
            go(v.tensor_scalar(s, ex, 2.0, None, ALU.add))
            go(v.reciprocal(s2, s))
            go(v.tensor_tensor(s, ex, s2, ALU.mult))
            go(v.tensor_tensor(s2, s, s, ALU.mult))
            TERMS = 9
            go(v.memset(acc, 1.0 / (2 * TERMS - 1)))
            for k in range(TERMS - 2, -1, -1):
                go(v.tensor_tensor(acc, acc, s2, ALU.mult))
                go(v.tensor_scalar(acc, acc, 1.0 / (2 * k + 1), None, ALU.add))
            go(v.scalar_tensor_tensor(acc, acc, 2.0, s, ALU.mult, ALU.mult))
            go(v.scalar_tensor_tensor(dt, u, 0.0, acc, ALU.max, ALU.add))
            go(v.tensor_tensor(as4(a), as4(dt), br(1), ALU.mult))
            go(v.tensor_scalar(a, a, -1.0, None, ALU.mult), "a_ready")
            dve.wait_ge(sem("conv_act"), NXB)
            dve.wait_ge(sem("bias_in"), 16)

            def heads(z):
                return z.rearrange("p (h c) -> p h c", h=SH)

            def per_head(z):
                return z.unsqueeze(2).to_broadcast([P, SH, SP])

            for c in range(NT):
                dtc = dt[:, c * SH:(c + 1) * SH]
                dve.wait_ge(sem("decays"), 3 * c + 2)
                go(v.tensor_tensor(sm[:, 4, :], ps[7][:, 8:16], sm[:, 0, :], ALU.subtract), "to_end")
                dve.wait_ge(sem("nat_sb"), 3 * c + 3)
                dve.wait_ge(sem("decays"), 3 * c + 3)
                go(v.tensor_tensor(heads(xdt), heads(xs), per_head(dtc), ALU.mult), "xdt")
                go(v.tensor_tensor(heads(xend), heads(xdt), per_head(sm[:, 3, :]), ALU.mult), "xend")
                for g in range(SG):
                    dve.wait_ge(sem("seg_ps"), SG * c + g + 1)
                    go(v.tensor_tensor(decay[:, g].rearrange("p (r l) -> p r l", r=SR),
                                       ps[2 + g][:].rearrange("p (r l) -> p r l", r=SR),
                                       sm[:, 0, SR * g:SR * g + SR].unsqueeze(2).to_broadcast([P, SR, P]),
                                       ALU.subtract), "seg_sb")
                for g in range(SG):
                    dve.wait_ge(sem("seg_exp"), SG * c + g + 1)
                    dg = decay[:, g].rearrange("p (r l) -> p r l", r=SR)
                    go(v.tensor_tensor(dg, dg, cbT[:, g * P:(g + 1) * P].unsqueeze(1).to_broadcast([P, SR, P]),
                                       ALU.mult), "lm_ready")
                dve.wait_ge(sem("y_ps"), c + 1)
                go(v.tensor_tensor(heads(y1), heads(xs), per_head(hrow[:, 2, :]), ALU.mult))
                go(v.tensor_tensor(y1, y1, ps[4][:], ALU.add))
                if c:
                    go(v.tensor_tensor(heads(y2), heads(ps[5][:]), per_head(sm[:, 1, :]), ALU.mult))
                    go(v.tensor_tensor(y1, y1, y2, ALU.add))
                    go(v.tensor_tensor(heads(state[:]), heads(state[:]), per_head(sm[:, 2, :]), ALU.mult))
                    go(v.tensor_tensor(state[:], state[:], ps[6][:], ALU.add), "state_ready")
                else:
                    go(v.tensor_copy(state[:], ps[6][:]), "state_ready")
                go(v.tensor_tensor(y1, y1, zs[:, c, :], ALU.mult))
                go(v.tensor_tensor_reduce(y2, y1, y1, 1.0, 0.0, ALU.mult, ALU.add, sm[:, 5, 0:1]))
                rms(sm[:, 5, 1:2], sm[:, 5, 0:1], 512, "dve_step")
                go(v.scalar_tensor_tensor(mix[:, 512:], y1, sm[:, 5, 1:2], wn[:], ALU.mult, ALU.mult), "y_done")
                k0 = 0 if c else P
                dve.wait_ge(sem("score_ps"), c + 1)
                for b in range(4):
                    src = ps[b][:].rearrange("p (h k) -> p h k", h=2)
                    go(v.scalar_tensor_tensor(prob[:, 2 * b:2 * b + 2, k0:], src[:, :, k0:], float(HD) ** -0.5,
                                              bias[:, 2 * b:2 * b + 2, k0:], ALU.mult, ALU.add), "score_sb")
                go(v.tensor_reduce(sm[:, 10, :], prob[:, :, k0:], AX.X, ALU.max))
                go(v.tensor_tensor(sm[:, 10, :], sm[:, 10, :], hrow[:, 3, :], ALU.max))
                go(v.tensor_tensor(sm[:, 7, :], hrow[:, 3, :], sm[:, 10, :], ALU.subtract))
                go(v.tensor_scalar(sm[:, 6, :], sm[:, 10, :], -1.0, None, ALU.mult), "neg_max")
                dve.wait_ge(sem("prob_exp"), 9 * c + 9)
                go(v.tensor_tensor(sm[:, 11, :], sm[:, 8, :], sm[:, 9, :], ALU.add))
                go(v.reciprocal(sm[:, 11, :], sm[:, 11, :]))
                dve.wait_ge(sem("pv_ps"), c + 1)
                go(v.tensor_tensor(heads(mix[:, 0:512]), heads(ps[0][:]), per_head(sm[:, 11, :]), ALU.mult), "mix_ready")
                dve.wait_ge(sem("wo_ps"), c + 1)
                go(v.tensor_tensor(h[:, c, 0:512], h[:, c, 0:512], ps[3][:], ALU.add))
                go(v.tensor_tensor(h[:, c, 512:], h[:, c, 512:], ps[4][:], ALU.add), "h_mixed")

            def top16(values, vals, where):
                go(v.max(vals[:, 0:8], values))
                go(v.max_index(where[:, 0:8], vals[:, 0:8], values))
                go(v.match_replace(values, vals[:, 0:8], values, LOWEST))
                go(v.max(vals[:, 8:16], values))
                go(v.max_index(where[:, 8:16], vals[:, 8:16], values))

            def route(t):
                dve.wait_ge(sem("wffn_in"), 32)
                dve.wait_ge(sem("sq_h"), t + 1)
                rms(ss[:, 8 + t:9 + t], ss[:, 4 + t:5 + t], D, "dve_step")
                if t >= 2:
                    dve.wait_ge(sem(f"stored{t - 2}"), 16)
                go(v.scalar_tensor_tensor(xn2[:, t % 2, :], h[:, t, :], ss[:, 8 + t:9 + t], w_ffn, ALU.mult, ALU.mult),
                   "xn2_ready")
                if t == 0:
                    go(v.tensor_copy(iota16, iota16i[:]))
                for j in range(2 * PH):
                    dve.wait_ge(sem("s_sb"), 4 * t + j // 4 + 1)
                    top16(score[:, j, :], val[:, j, :], vidx[:, j, :])
                go(v.tensor_copy(vidf, vidx))
                v4 = val.rearrange("p (h s) k -> p h s k", s=2)
                f4 = vidf.rearrange("p (h s) k -> p h s k", s=2)
                for hh in range(PH):
                    go(v.tensor_tensor(cand[:, hh, :].rearrange("p (a b) -> p a b", a=TOPK),
                                       v4[:, hh, 0, :].unsqueeze(2).to_broadcast([P, TOPK, TOPK]),
                                       v4[:, hh, 1, :].unsqueeze(1).to_broadcast([P, TOPK, TOPK]), ALU.add))
                    top16(cand[:, hh, :], top[:, hh, :], tpos[:, hh, :])
                go(v.tensor_scalar(tab[:, 0, :], tpos.rearrange("p h k -> p (h k)"), 4, None, ALU.logical_shift_right))
                go(v.tensor_scalar(tab[:, 1, :], tpos.rearrange("p h k -> p (h k)"), 15, None, ALU.bitwise_and))
                go(v.tensor_copy(tabf[:, 0:2, :], tab))
                for s_ in range(2):
                    pos4 = tabf[:, s_, :].rearrange("p (h k) -> p h k", h=PH)
                    for hh in range(PH):
                        go(v.tensor_tensor(hit4[:, hh], pos4[:, hh].unsqueeze(2).to_broadcast([P, TOPK, TOPK]),
                                           iota16.unsqueeze(1).to_broadcast([P, TOPK, TOPK]), ALU.is_equal))
                        go(v.tensor_tensor(hit4[:, hh], hit4[:, hh],
                                           f4[:, hh, s_, :].unsqueeze(1).to_broadcast([P, TOPK, TOPK]), ALU.mult))
                    go(v.tensor_reduce(tabf[:, 2 + s_, :], hit.rearrange("p (m a) -> p m a", a=TOPK), AX.X, ALU.add),
                       "route_mid" if s_ else "dve_step")
                go(v.scalar_tensor_tensor(tabf[:, 0, :], tabf[:, 2, :], float(NK), tabf[:, 3, :], ALU.mult, ALU.add))
                go(v.tensor_copy(idx[:, t % 2, :], tabf[:, 0, :]))
                hk = lambda z: z.rearrange("p (h k) -> p h k", h=PH)
                go(v.tensor_tensor(hk(tabf[:, 2, :]), top, top[:, :, 0:1].to_broadcast([P, PH, TOPK]), ALU.subtract),
                   "gate_in")
                dve.wait_ge(sem("gate_exp"), t + 1)
                go(v.tensor_reduce(gsum[:, 0, :], hk(tabf[:, 3, :]), AX.X, ALU.add))
                go(v.reciprocal(gsum[:, 1, :], gsum[:, 0, :]))
                go(v.tensor_tensor(hk(gate[:, t % 2, :]), hk(tabf[:, 3, :]),
                                   gsum[:, 1, :].unsqueeze(2).to_broadcast([P, PH, TOPK]), ALU.mult), "routed")

            def experts(t):
                with dve.Fori(0, SLOTS // GROUP // 2) as r:
                    for half in range(2):
                        g0 = t * (SLOTS // GROUP) + half
                        for i in range(GROUP):
                            dve.wait_ge(sem(f"down{i}"), 16 * (g0 + 2 * r) + 16)
                            v.tensor_tensor_reduce(down[:, i, :], down[:, i, :], xn2[:, t % 2, :], 1.0, 0.0,
                                                   ALU.mult, ALU.add, pre[:, half, i:i + 1]).then_inc(sem("dots"), 1)
                        dve.wait_ge(sem("gelu"), g0 + 2 * r + 1)
                        dve.wait_ge(sem("gnow_ready"), g0 + 2 * r + 1)
                        v.tensor_tensor(actv[:, half], gel[:, half], gnow[:, half], ALU.mult
                                        ).then_inc(sem("act_ready"), 1)
                final = xn2[:, t % 2, :]
                dve.wait_ge(sem("fin_sq"), 2 * t + 2)
                go(v.tensor_tensor(ss[:, 14:15], ss[:, 12:13], ss[:, 13:14], ALU.add))
                rms(ss[:, 15:16], ss[:, 14:15], D, "dve_step")
                go(v.scalar_tensor_tensor(final[:, 0:512], ps[6][:], ss[:, 15:16], w_fin[:, 0:512], ALU.mult, ALU.mult))
                go(v.scalar_tensor_tensor(final[:, 512:], ps[7][:], ss[:, 15:16], w_fin[:, 512:], ALU.mult, ALU.mult),
                   "final_ready")

            for t in range(NT):
                route(t)
                experts(t)

        @block.tensor
        def _(pe):
            mm = nc.tensor.matmul
            pe.wait_ge(sem("const"), LOADS["const"])
            for t in range(NT):
                pe.wait_ge(sem("xn_ready"), t + 1)
                if t >= 2:
                    pe.wait_ge(sem("xT_sb"), 2 * (t - 1))
                for k in range(KT):
                    last = nc.tensor.transpose(ps[2 * (t % 2) + k // 4][:, (k % 4) * P:(k % 4 + 1) * P],
                                               xn[:, t % 2, k * P:(k + 1) * P], ident[:])
                last.then_inc(sem("xT_ps"), 1)
            pe.wait_ge(sem("line_in"), 32)
            pe.wait_ge(sem("rb_ones"), 1)
            for hh in range(HEADS):
                if hh >= 2:
                    pe.wait_ge(sem("line_done"), hh - 1)
                mm(ps[4 + hh % 2][:, 0:LW], rb[:, hh:hh + 1].to_broadcast([N_BUCKETS + 1, P]), buckets,
                   start=True, stop=True).then_inc(sem("line_ps"), 1)
            pe.wait_ge(sem("xT_sb"), 2 * NT)
            for b in range(NBLK):
                pe.wait_ge(sem(f"ring{b % RING}"), 16 * (b // RING + 1))
                if b >= 4:
                    pe.wait_ge(sem("proj_out"), b - 3)
                w = ring[:, b % RING]
                if b < B_V:
                    for k in range(KT):
                        last = mm(ps[b % 4][:], w[:, k, :], xnT[:, k, :], start=(k == 0), stop=(k == KT - 1))
                else:
                    for t in range(NT):
                        for k in range(KT):
                            last = mm(ps[b % 4][:, t * P:(t + 1) * P], xnT[:, k, t * P:(t + 1) * P], w[:, k, :],
                                      start=(k == 0), stop=(k == KT - 1))
                last.then_inc(sem("block_used"), 1)
            pe.wait_ge(sem("wdt_in"), 16)
            pe.wait_ge(sem("proj_out"), NBLK - 3)
            for t in range(NT):
                for k in range(KT):
                    last = mm(ps[NBLK % 4][:, t * SH:(t + 1) * SH], xnT[:, k, t * P:(t + 1) * P], w_dt_sb[:, k, :],
                              start=(k == 0), stop=(k == KT - 1))
            last.then_inc(sem("block_used"), 1)

            pe.wait_ge(sem("proj_out"), NBLK + 1)
            pe.wait_ge(sem("conv_act"), NXB)
            pe.wait_ge(sem("a_ready"), 1)
            a = dtv[:, 7, :]
            for c in range(NT):
                tc = slice(c * P, (c + 1) * P)
                if c:
                    pe.wait_ge(sem("h_mixed"), c)
                ac = a[:, c * SH:(c + 1) * SH]
                mm(ps[7][:, 0:8], tri[:], ac, start=True, stop=True)
                mm(ps[7][:, 8:16], ones[:], ac, start=True, stop=True).then_inc(sem("acum_ps"), 1)
                for j in range(4):
                    nc.tensor.transpose(ps[0][:, j * P:(j + 1) * P], xconv[:, j, tc], ident[:])
                for g in range(SG):
                    nc.tensor.transpose(ps[1][:, g * P:(g + 1) * P], xconv[:, 4 + g, tc], ident[:])
                for g in range(SG):
                    last = mm(ps[1][:, (2 + g) * P:(3 + g) * P], xconv[:, 4 + g, tc], xconv[:, 6 + g, tc],
                              start=True, stop=True)
                last.then_inc(sem("nat_ps"), 1)
                for g in range(SG):
                    bank = ps[2 + g][:].rearrange("p (r l) -> p r l", r=SR)
                    mm(bank, ident[:], negm[:].unsqueeze(1).to_broadcast([P, SR, P]), start=True, stop=False,
                       skip_group_check=True)
                    for r in range(SR):
                        hh = g * SR + r
                        last = mm(bank[:, r, :], ac[:, hh:hh + 1].to_broadcast([P, P]), tri[:], start=False,
                                  stop=(r == SR - 1), skip_group_check=True)
                    last.then_inc(sem("seg_ps"), 1)
                if c:
                    pe.wait_ge(sem("state_ready"), c)
                    for g in range(SG):
                        mm(ps[5][:, g * 256:(g + 1) * 256], xconv[:, 6 + g, tc], state[:, g * 256:(g + 1) * 256],
                           start=True, stop=True)
                pe.wait_ge(sem("xend"), c + 1)
                for g in range(SG):
                    mm(ps[6][:, g * 256:(g + 1) * 256], bnat[:, g * P:(g + 1) * P], xend[:, g * 256:(g + 1) * 256],
                       start=True, stop=True)
                pe.wait_ge(sem("lm_ready"), SG * (c + 1))
                for hh in range(SH):
                    last = mm(ps[4][:, hh * SP:(hh + 1) * SP], decay[:, hh // SR, (hh % SR) * P:(hh % SR + 1) * P],
                              xdt[:, hh * SP:(hh + 1) * SP], start=True, stop=True)
                last.then_inc(sem("y_ps"), 1)
                k0 = 0 if c else P
                for hh in range(HEADS):
                    half = slice(HD * (hh // 4), HD * (hh // 4) + HD)
                    last = mm(ps[hh // 2][:, (hh % 2) * 256 + k0:(hh % 2) * 256 + 256],
                              qkT[half, 1 + hh % 4, tc], qkT[half, 0, c * P - P + k0:(c + 1) * P], start=True, stop=True)
                last.then_inc(sem("score_ps"), 1)
                pe.wait_ge(sem("prob_exp"), 9 * c + 9)
                pe.wait_ge(sem("y_done"), c + 1)
                for hh in range(HEADS):
                    for kb in range(0 if c else 1, 2):
                        last = nc.tensor.transpose(ps[4 + hh // 2][:, ((hh % 2) * 2 + kb) * P:((hh % 2) * 2 + kb + 1) * P],
                                                   prob[:, hh, kb * P:(kb + 1) * P], ident[:])
                last.then_inc(sem("pt_ps"), 1)
                pe.wait_ge(sem("pt_sb"), 4 * c + 4)
                for hh in range(HEADS):
                    for kb in range(0 if c else 1, 2):
                        i = (hh % 2) * 2 + kb
                        last = mm(ps[0][:, hh * HD:(hh + 1) * HD], probT[:, hh // 2, i * P:(i + 1) * P],
                                  v_sb[:, c - 1 + kb, (hh // 4) * HD:(hh // 4 + 1) * HD], start=(kb == 0 or c == 0),
                                  stop=(kb == 1))
                last.then_inc(sem("pv_ps"), 1)
                pe.wait_ge(sem("mix_ready"), c + 1)
                for k in range(KT):
                    last = nc.tensor.transpose(ps[1 + k // 4][:, (k % 4) * P:(k % 4 + 1) * P], mix[:, k * P:(k + 1) * P],
                                               ident[:])
                last.then_inc(sem("mixT_ps"), 1)
                pe.wait_ge(sem("mixT_sb"), 2 * c + 2)
                pe.wait_ge(sem("wo_in"), 16)
                for b in range(2):
                    for k in range(KT):
                        last = mm(ps[3 + b][:], mixT[:, k, :], wo[:, k, b * 512:(b + 1) * 512], start=(k == 0),
                                  stop=(k == KT - 1))
                last.then_inc(sem("wo_ps"), 1)

            def route(t):
                pe.wait_ge(sem("xn2_ready"), t + 1)
                for k in range(KT):
                    last = nc.tensor.transpose(ps[k // 4][:, (k % 4) * P:(k % 4 + 1) * P],
                                               xn2[:, t % 2, k * P:(k + 1) * P], ident[:])
                last.then_inc(sem("xn2T_ps"), 1)
                pe.wait_ge(sem("xn2T_sb"), 2 * t + 2)
                pe.wait_ge(sem("wq_in"), 48)
                for b in range(4):
                    if b >= 2:
                        pe.wait_ge(sem("q_sb"), 4 * t + b - 1)
                    for j in range(4):
                        for k in range(KT):
                            col = (4 * b + j) * P
                            last = mm(ps[2 + b % 2][:, j * P:(j + 1) * P], wq[:, k, col:col + P], xn2T[:, k, :],
                                      start=(k == 0), stop=(k == KT - 1))
                    last.then_inc(sem("q_ps"), 1)
                for b in range(4):
                    pe.wait_ge(sem("q_sb"), 4 * t + b + 1)
                    if b >= 2:
                        pe.wait_ge(sem("s_sb"), 4 * t + b - 1)
                    for j in range(4):
                        last = mm(ps[b % 2][:, j * P:(j + 1) * P], qT[:, 4 * b + j, :], keysT[:, j % 2, :],
                                  start=True, stop=True)
                    last.then_inc(sem("s_ps"), 1)

            def experts(t):
                if t:
                    pe.wait_ge(sem("final_ready"), t)
                else:
                    pe.wait_ge(sem("h_mixed"), NT)
                for b in range(2):
                    mm(ps[6 + b][:], ident[:], h[:, t, b * 512:(b + 1) * 512], start=True, stop=False,
                       skip_group_check=True)
                with pe.Fori(0, SLOTS // GROUP // 2) as r:
                    for half in range(2):
                        g0 = t * (SLOTS // GROUP) + half
                        for i in range(GROUP):
                            pe.wait_ge(sem("diag"), 8 * (g0 + 2 * r) + i + 1)
                            pe.wait_ge(sem(f"up{i}"), 16 * (g0 + 2 * r) + 16)
                            mm(ps[6][:], diag[:, i, :], up[:, i, 0:512], start=False, stop=False,
                               skip_group_check=True)
                            mm(ps[7][:], diag[:, i, :], up[:, i, 512:], start=False, stop=False,
                               skip_group_check=True).then_inc(sem("up_free"), 1)
                pe.wait_ge(sem("up_free"), 8 + SLOTS * (t + 1))
                pe.nop(nofuse=True).then_inc(sem("peer_done"), 1)

            for t in range(NT):
                route(t)
                experts(t)


def bucket_lines():
    dist = P + P - 1 - np.arange(LW)
    n = np.maximum(dist, 0)
    exact = N_BUCKETS // 2
    nf = np.maximum(n, 1).astype(np.float32)
    large = exact + (np.log(nf / np.float32(exact)) / np.float32(math.log(MAX_DISTANCE / exact))
                     * np.float32(N_BUCKETS - exact)).astype(np.int32)
    large = np.minimum(large, N_BUCKETS - 1)
    which = np.where(n < exact, n, large)
    ok = (dist >= 0) & (dist < WINDOW)
    lines = np.zeros((N_BUCKETS + 1, LW), np.float32)
    lines[which[ok], np.nonzero(ok)[0]] = 1.0
    lines[N_BUCKETS, ~ok] = NEG
    return lines


def kernel(**inputs):
    import numpy as _np
    import concourse.bacc as _bacc
    from concourse import mybir as _mybir
    from concourse.bass_utils import run_bass_kernel_spmd as _run

    g = {k: _np.asarray(a) for k, a in inputs.items()}
    w = g["w_in"][0]
    kv = HEADS * HD
    off_v, off_z = kv + KV_HEADS * HD, kv + 2 * KV_HEADS * HD
    off_x = off_z + SH * SP
    off_dt = off_x + XBC
    cols = [_np.arange(off_x + j * P, off_x + (j + 1) * P) for j in range(NXB)]
    cols += [_np.arange(kv, off_v)]
    cols += [_np.concatenate([_np.arange(j * HD, (j + 1) * HD), _np.arange((4 + j) * HD, (5 + j) * HD)]) for j in range(4)]
    cols += [_np.arange(off_v, off_z)]
    cols += [_np.arange(off_z + j * P, off_z + (j + 1) * P) for j in range(4)]

    def by_rows(m):
        return _np.ascontiguousarray(m.reshape(KT, P, m.shape[1]).transpose(1, 0, 2).reshape(P, -1))

    host = {
        "x": g["x"], "w_in_blocks": _np.stack([by_rows(w[:, c]) for c in cols]), "w_dt": by_rows(w[:, off_dt:]),
        "norm_mix": g["norm_mix"][0].reshape(KT, P).T,
        "conv_w": g["conv_w"][0].reshape(CONV, NXB, P).transpose(2, 0, 1), "conv_b": g["conv_b"][0].reshape(NXB, P).T,
        "dt_bias": g["dt_bias"],
        "a_log": g["a_log"], "d_skip": g["d_skip"], "ssd_norm_w": g["ssd_norm_w"], "sinks": g["attn_sinks"],
        "w_out": g["w_out"][0], "rel_bias": g["rel_bias"], "bucket_line": bucket_lines(), "norm_ffn": g["norm_ffn"],
        "w_query": g["w_query"][0], "keys1_t": g["sub_keys1"][0].T, "keys2_t": g["sub_keys2"][0].T,
        "expert_down": g["expert_down"][0], "expert_up": g["expert_up"][0], "norm_final": g["norm_final"][None],
    }
    nc = _bacc.Bacc("TRN2", target_bir_lowering=False, num_devices=1)
    arrays, args = {}, []
    for name, a in host.items():
        a = _np.ascontiguousarray(a)
        arrays[f"in_{name}_dram"] = a
        args.append(nc.dram_tensor(f"in_{name}_dram", a.shape, _mybir.dt.from_np(a.dtype), kind="ExternalInput").ap())
    out = nc.dram_tensor("out_0_dram", (1, SEQ, D), F32, kind="ExternalOutput").ap()
    layer(nc, *args, out)
    r = _run(nc, [arrays], core_ids=[0])
    return r.results[0]["out_0_dram"]
```

```python
import math
from contextlib import ExitStack

import numpy as np

import concourse.bass as bass
from concourse import mybir

ALU = mybir.AluOpType
ACT = mybir.ActivationFunctionType
AX = mybir.AxisListType
F32 = mybir.dt.float32
I32 = mybir.dt.int32
U32 = mybir.dt.uint32

P = 128
D = 1024
KT = D // P
SEQ = 512
NT = SEQ // P
HEADS, KV_HEADS, HD = 8, 2, 64
WINDOW = 128
N_BUCKETS, MAX_DISTANCE = 32, 128
SH, SP, SN, SG = 8, 64, 128, 2
SR = SH // SG
CONV = 4
XBC = SH * SP + 2 * SG * SN
NXB = XBC // P
PH, NK, TOPK = 8, 128, 16
SLOTS = PH * TOPK
GROUP = 8
EPS = 1e-6
NEG = -1e30
LOWEST = -3.0e38
LW = 3 * P
NBLK = NXB + 5 + 1 + 4
RING = 5
B_K, B_Q, B_V, B_Z = NXB, NXB + 1, NXB + 5, NXB + 6


def layer(nc, x, w_in_blocks, w_dt, norm_mix, conv_w, conv_b, dt_bias, a_log, d_skip, ssd_norm_w, sinks, w_out,
          rel_bias, bucket_line, norm_ffn, w_query, keys1_t, keys2_t, expert_down, expert_up, norm_final, out):
    line_dram = nc.dram_tensor("line_scratch", (P, HEADS * LW), F32, kind="Internal").ap()
    with ExitStack() as ctx:
        def sb(name, shape, dt=F32):
            return ctx.enter_context(nc.sbuf_tensor(name, shape, dt))

        SEMS = {}

        def sem(name):
            if name not in SEMS:
                SEMS[name] = ctx.enter_context(nc.semaphore(name))
            return SEMS[name]

        arena = sb("arena", [P, 24 * D])
        arena2 = sb("arena2", [P, 6 * D])
        wq = sb("wq", [P, KT, PH * 2 * P])
        h = sb("h", [P, NT, D])

        def slot(i, n=1, of=arena):
            return of[:, i * D:(i + n) * D]

        xnT = slot(0, 4).rearrange("p (k t) -> p k t", k=KT)
        ring = slot(4, RING).rearrange("p (s k c) -> p s k c", s=RING, k=KT)
        PAD = CONV - 1
        xraw = arena[:, 9 * D:9 * D + NXB * (SEQ + PAD)].rearrange("p (j t) -> p j t", j=NXB)
        xconv = slot(14, 4).rearrange("p (j t) -> p j t", j=NXB)
        zs = slot(18, 2).rearrange("p (t c) -> p t c", t=NT)
        qkT = arena[:, 20 * D:20 * D + 5 * SEQ].rearrange("p (j t) -> p j t", j=5)
        v_sb = arena[:, 23 * D:23 * D + NT * P].rearrange("p (t c) -> p t c", t=NT)
        wo = slot(0, 8).rearrange("p (k c) -> p k c", k=KT)
        bias = slot(0, 2, arena2).rearrange("p (h k) -> p h k", h=HEADS)
        prob = slot(2, 2, arena2).rearrange("p (h k) -> p h k", h=HEADS)
        probT = slot(4, 2, arena2).rearrange("p (b c) -> p b c", b=4)
        xn = slot(4, 2, arena2).rearrange("p (b c) -> p b c", b=2)
        line = arena[:, 14 * D:14 * D + HEADS * LW].rearrange("p (h m) -> p h m", h=HEADS)
        buckets = arena[0:N_BUCKETS + 1, 18 * D:18 * D + LW]
        xs = slot(9)[:, 0:512]
        xdt = slot(9)[:, 512:1024]
        xend = slot(10)[:, 0:512]
        bnat = slot(10)[:, 512:768]
        cbT = slot(10)[:, 768:1024]
        decay = slot(11).rearrange("p (g c) -> p g c", g=SG)
        mix = slot(12)
        mixT = slot(13).rearrange("p (k t) -> p k t", k=KT)
        y1 = arena[:, 23 * D + 512:24 * D]
        y2 = arena[:, 22 * D + 512:23 * D]
        down = slot(0, 8).rearrange("p (s c) -> p s c", s=8)
        up = slot(8, 8).rearrange("p (s c) -> p s c", s=8)
        xn2 = slot(16, 2).rearrange("p (b c) -> p b c", b=2)
        xn2T = slot(18).rearrange("p (k t) -> p k t", k=KT)
        one = slot(19)
        pair = one[:, 0:256].rearrange("p (s n) -> p s n", s=2)
        sums = one[:, 256:512]
        pval = one[:, 512:544].rearrange("p (s k) -> p s k", s=2)
        pidx = one[:, 544:576].bitcast(U32).rearrange("p (s k) -> p s k", s=2)
        pidf = one[:, 576:608].rearrange("p (s k) -> p s k", s=2)
        tval = one[:, 608:624]
        tpos = one[:, 624:640].bitcast(U32)
        digit = one[:, 640:672].bitcast(U32).rearrange("p (s k) -> p s k", s=2)
        digf = one[:, 672:704].rearrange("p (s k) -> p s k", s=2)
        part = one[:, 704:736].rearrange("p (s k) -> p s k", s=2)
        pick = one[:, 736:752]
        score = slot(21, 2).rearrange("p (j n) -> p j n", j=2 * PH)
        hit = slot(23)[:, 0:512].rearrange("p (s k a) -> p s k a", s=2, k=TOPK)
        qT = slot(0, 2, arena2).rearrange("p (j t) -> p j t", j=2 * PH)
        diag = slot(2, 1, arena2).rearrange("p (s c) -> p s c", s=GROUP)
        w_ffn = slot(3, 1, arena2)
        w_fin = slot(4, 1, arena2)
        keep = slot(5, 1, arena2)
        idx = keep[:, 0:256].bitcast(I32).rearrange("p (b m) -> p b m", b=2)
        gate = keep[:, 256:512].rearrange("p (b m) -> p b m", b=2)
        keysT = keep[:, 512:768].rearrange("p (s n) -> p s n", s=2)

        ident = sb("ident", [P, P])
        tri = sb("tri", [P, P])
        negm = sb("negm", [P, P])
        ones = sb("ones", [P, P])
        state = sb("state", [P, 512])
        wn = sb("wn", [P, 512])
        wmix = sb("wmix", [P, KT])
        early = slot(2, 1, arena2)
        w_dt_sb = early[:, 0:64].rearrange("p (k c) -> p k c", k=KT)
        cw = early[:, 64:96].rearrange("p (w j) -> p w j", w=CONV)
        cb = early[:, 96:104]
        rb = sb("rb", [N_BUCKETS + 1, HEADS])
        hrow = sb("hrow", [P, 4, SH])
        ss = sb("ss", [P, 16])
        dtv = sb("dtv", [P, 8, NT * SH])
        sm = sb("sm", [P, 12, SH])
        top = slot(23)[:, 512:640].rearrange("p (h k) -> p h k", h=PH)
        wide = slot(20)
        eg = slot(23)[:, 640:768]
        iota16 = keep[:, 856:872]
        iota16i = sb("iota16i", [P, TOPK], I32)
        gsum = keep[:, 832:856].rearrange("p (i h) -> p i h", i=3)
        inow = keep[:, 768:784].bitcast(I32).rearrange("p (b i) -> p b i", b=2)
        gnow, pre, gel = (keep[:, 784 + 16 * i:800 + 16 * i].rearrange("p (b i) -> p b i", b=2) for i in range(3))
        sq = sb("sq", [P, 2])
        actv = sb("actv", [P, 2, GROUP])

        ps = [ctx.enter_context(nc.psum_tensor(f"ps{i}", [P, 512], F32)) for i in range(8)]

        block = ctx.enter_context(nc.Block())

        def link(eng, ins, name, count):
            count[name] = count.get(name, 0) + 1
            ins.then_inc(sem(name), 1)
            eng.wait_ge(sem(name), count[name])

        LOADS = {}

        @block.sync
        def _(sp):
            for t in range(NT):
                sp.dma_start(h[:, t, :], x[0, t * P:(t + 1) * P, :]).then_inc(sem(f"x_in{t}"), 16)
                if t == 0:
                    sp.dma_start(buckets, bucket_line).then_inc(sem("line_in"), 16)
                    sp.dma_start(rb[0:N_BUCKETS, :], rel_bias).then_inc(sem("line_in"), 16)
                    sp.dma_start(wmix[:], norm_mix).then_inc(sem("wmix_in"), 16)
            for b in range(NBLK):
                if b >= RING:
                    sp.wait_ge(sem("block_used"), b - RING + 1)
                sp.dma_start(ring[:, b % RING], w_in_blocks[b].rearrange("p (k c) -> p k c", k=KT)
                             ).then_inc(sem(f"ring{b % RING}"), 16)
                if b == 2:
                    sp.dma_start(cw, conv_w).then_inc(sem("conv_in"), 16)
                    sp.dma_start(cb, conv_b).then_inc(sem("conv_in"), 16)
                if b == 4:
                    sp.dma_start(w_dt_sb, w_dt.rearrange("p (k c) -> p k c", k=KT)).then_inc(sem("wdt_in"), 16)
                    for i, row in enumerate((dt_bias, a_log, d_skip, sinks)):
                        sp.dma_start(hrow[:, i, :], row.to_broadcast([P, SH])).then_inc(sem("rows_in"), 16)
                    sp.dma_start(wn[:], ssd_norm_w.to_broadcast([P, 512])).then_inc(sem("rows_in"), 16)
                    sp.wait_ge(sem("line_done"), HEADS)
                    sp.dma_start(line_dram, line).then_inc(sem("line_out"), 16)
                    sp.wait_ge(sem("line_out"), 16)
                    skew = bass.AP(line_dram.tensor, P - 1, [[HEADS * LW - 1, P], [LW, HEADS], [1, 2 * P]])
                    sp.dma_start(bias, skew).then_inc(sem("bias_in"), 16)
            sp.wait_ge(sem("block_used"), NBLK + 1)
            sp.dma_start(wo, w_out.rearrange("(k p) c -> p k c", p=P)).then_inc(sem("wo_in"), 16)
            sp.dma_start(wq[:], w_query.rearrange("(k p) c -> p k c", p=P)).then_inc(sem("wq_in"), 16)
            sp.wait_ge(sem("h_mixed"), NT)
            sp.dma_start(keysT[:, 0, :], keys1_t).then_inc(sem("wq_in"), 16)
            sp.dma_start(keysT[:, 1, :], keys2_t).then_inc(sem("wq_in"), 16)
            sp.dma_start(w_ffn, norm_ffn.to_broadcast([P, D])).then_inc(sem("wffn_in"), 16)
            sp.dma_start(w_fin, norm_final.to_broadcast([P, D])).then_inc(sem("wffn_in"), 16)
            for t in range(NT):
                sp.wait_ge(sem("final_ready"), t + 1)
                sp.dma_start(out[0, t * P:(t + 1) * P, :], xn2[:, t % 2, :]).then_inc(sem(f"stored{t}"), 16)
            for t in range(NT):
                sp.wait_ge(sem(f"stored{t}"), 16)

        @block.gpsimd
        def _(gp):
            n = {}
            link(gp, gp.memset(ones[:], 1.0), "const", n)
            link(gp, gp.memset(negm[:], 0.0), "const", n)
            link(gp, gp.affine_select(out=ident[:], in_=ones[:], compare_op=ALU.is_equal, fill=0.0, base=0,
                                      pattern=[[-1, P]], channel_multiplier=1), "const", n)
            link(gp, gp.affine_select(out=tri[:], in_=ones[:], compare_op=ALU.is_ge, fill=0.0, base=0,
                                      pattern=[[1, P]], channel_multiplier=-1), "const", n)
            link(gp, gp.affine_select(out=negm[:], in_=negm[:], compare_op=ALU.is_ge, fill=NEG, base=0,
                                      pattern=[[1, P]], channel_multiplier=-1), "const", n)
            link(gp, gp.iota(iota16i[:], pattern=[[1, TOPK]], base=0, channel_multiplier=0), "const", n)
            for j in range(NXB):
                link(gp, gp.memset(xraw[:, j, 0:PAD], 0.0), "const", n)
            LOADS["const"] = n["const"]
            for t in range(NT):
                gp.wait_ge(sem("routed"), t + 1)
                with gp.Fori(0, SLOTS // GROUP // 2) as r:
                    for half in range(2):
                        g0 = t * (SLOTS // GROUP) + half
                        if half == 0:
                            gp.wait_ge(sem("up_free"), 8 * (g0 + 2 * r) + 1)
                        gp.tensor_copy(inow[:, half], idx[:, t % 2, bass.ds((2 * r + half) * GROUP, GROUP)]
                                       ).then_inc(sem("inow_ready"), 1)
                        gp.tensor_copy(gnow[:, half], gate[:, t % 2, bass.ds((2 * r + half) * GROUP, GROUP)]
                                       ).then_inc(sem("gnow_ready"), 1)
                        gp.wait_ge(sem("inow_ready"), g0 + 2 * r + 1)
                        for i in range(GROUP):
                            gp.wait_ge(sem("dots"), 8 * (g0 + 2 * r) + i + 1)
                            gp.nop(nofuse=True)
                            gp.indirect_dma_start(down[:, i, :], None, expert_down,
                                                  bass.IndirectOffsetOnAxis(ap=inow[:, half, i:i + 1], axis=0)
                                                  ).then_inc(sem(f"down{i}"), 16)
                        for i in range(GROUP):
                            gp.wait_ge(sem("up_free"), 8 * (g0 + 2 * r) + i + 1)
                            gp.nop(nofuse=True)
                            gp.indirect_dma_start(up[:, i, :], None, expert_up,
                                                  bass.IndirectOffsetOnAxis(ap=inow[:, half, i:i + 1], axis=0)
                                                  ).then_inc(sem(f"up{i}"), 16)

        @block.scalar
        def _(act):
            n = {}

            def copy(o, i, name="act_step", func=ACT.Copy, **kw):
                link(act, nc.scalar.activation(o, i, func, **kw), name, n)

            for t in range(NT):
                act.wait_ge(sem(f"x_in{t}"), 16)
                if t:
                    act.wait_ge(sem("xn_ready"), t)
                copy(slot(19), h[:, t, :], "sq_x", ACT.Square, accum_out=ss[:, t:t + 1])
            for hh in range(HEADS):
                act.wait_ge(sem("line_ps"), hh + 1)
                copy(line[:, hh, :], ps[4 + hh % 2][:, 0:LW], "line_done")
            for b in range(NBLK + 1):
                act.wait_ge(sem("block_used"), b + 1)
                src = ps[b % 4]
                if b < NXB:
                    copy(xraw[:, b, PAD:], src[:], "proj_out")
                elif b < B_V:
                    copy(qkT[:, b - B_K, :], src[:], "proj_out")
                elif b == B_V:
                    copy(v_sb, src[:].rearrange("p (t c) -> p t c", t=NT), "proj_out")
                elif b < NBLK:
                    copy(zs[:, :, (b - B_Z) * P:(b - B_Z + 1) * P], src[:].rearrange("p (t c) -> p t c", t=NT),
                         "proj_out", ACT.Silu)
                else:
                    copy(dtv[:, 0, :], src[:, 0:NT * SH], "proj_out")
            act.wait_ge(sem("conv_in"), 32)
            for j in range(NXB):
                act.wait_ge(sem("conv_done"), j + 1)
                copy(xconv[:, j, :], xconv[:, j, :], "conv_act", ACT.Silu, bias=cb[:, j:j + 1])
            act.wait_ge(sem("dt_abs"), 1)
            copy(dtv[:, 2, :], dtv[:, 1, :], "dt_exp", ACT.Exp, scale=-1.0)
            copy(hrow[:, 1, :], hrow[:, 1, :], "dt_exp", ACT.Exp)

            for c in range(NT):
                act.wait_ge(sem("acum_ps"), c + 1)
                if c:
                    act.wait_ge(sem("y_done"), c)
                copy(sm[:, 0, :], ps[7][:, 0:8], "acum_sb")
                copy(sm[:, 1, :], ps[7][:, 0:8], "decays", ACT.Exp)
                copy(sm[:, 2, :], ps[7][:, 8:16], "decays", ACT.Exp)
                act.wait_ge(sem("to_end"), c + 1)
                copy(sm[:, 3, :], sm[:, 4, :], "decays", ACT.Exp)
                act.wait_ge(sem("nat_ps"), c + 1)
                copy(xs, ps[0][:], "nat_sb")
                copy(bnat, ps[1][:, 0:256], "nat_sb")
                copy(cbT, ps[1][:, 256:512], "nat_sb")
                for g in range(SG):
                    act.wait_ge(sem("seg_sb"), SG * c + g + 1)
                    copy(decay[:, g], decay[:, g], "seg_exp", ACT.Exp)
                act.wait_ge(sem("neg_max"), c + 1)
                if c:
                    act.wait_ge(sem("pt_ps"), c)
                k0 = 0 if c else P
                for hh in range(HEADS):
                    copy(prob[:, hh, k0:], prob[:, hh, k0:], "prob_exp", ACT.Exp, bias=sm[:, 6, hh:hh + 1],
                         accum_out=sm[:, 8, hh:hh + 1])
                copy(sm[:, 9, :], sm[:, 7, :], "prob_exp", ACT.Exp)
                for b in range(4):
                    if c:
                        act.wait_ge(sem("pt_ps"), c + 1)
                        copy(probT[:, b, :], ps[4 + b][:], "pt_sb")
                    else:
                        act.wait_ge(sem("pt_ps"), c + 1)
                        half = ps[4 + b][:].rearrange("p (i q) -> p i q", i=4)[:, 1::2, :]
                        copy(probT[:, b, :].rearrange("p (i q) -> p i q", i=4)[:, 1::2, :], half, "pt_sb")
                act.wait_ge(sem("mixT_ps"), c + 1)
                for b in range(2):
                    copy(mixT[:, 4 * b:4 * b + 4, :], ps[1 + b][:].rearrange("p (k t) -> p k t", k=4), "mixT_sb")

            def score_keys(t):
                if t == 0:
                    act.wait_ge(sem("h_mixed"), NT)
                copy(wide, h[:, t, :], "sq_h", ACT.Square, accum_out=ss[:, 4 + t:5 + t])
                act.wait_ge(sem("xn2T_ps"), t + 1)
                for b in range(2):
                    copy(xn2T[:, 4 * b:4 * b + 4, :], ps[b][:].rearrange("p (k t) -> p k t", k=4), "xn2T_sb")
                for b in range(4):
                    act.wait_ge(sem("q_ps"), 4 * t + b + 1)
                    copy(qT[:, 4 * b:4 * b + 4, :], ps[2 + b % 2][:].rearrange("p (j t) -> p j t", j=4), "q_sb")
                if t:
                    act.wait_ge(sem("gate_in"), t)
                for b in range(4):
                    act.wait_ge(sem("s_ps"), 4 * t + b + 1)
                    copy(score[:, 4 * b:4 * b + 4, :], ps[b % 2][:].rearrange("p (j t) -> p j t", j=4), "s_sb")

            def softmax_exp(t):
                act.wait_ge(sem("gate_in"), t + 1)
                copy(eg, eg, "gate_exp", ACT.Exp)

            def experts(t):
                with act.Fori(0, SLOTS // GROUP // 2) as r:
                    for half in range(2):
                        g0 = t * (SLOTS // GROUP) + half
                        act.wait_ge(sem("dots"), 8 * (g0 + 2 * r) + 16)
                        nc.scalar.activation(gel[:, half], pre[:, half], ACT.Gelu).then_inc(sem("gelu"), 1)
                        act.wait_ge(sem("act_ready"), g0 + 2 * r + 1)
                        for i in range(GROUP):
                            act.wait_ge(sem("up_free"), 8 * (g0 + 2 * r) + i + 1)
                            nc.scalar.activation(diag[:, i, :], ident[:], ACT.Copy, scale=actv[:, half, i:i + 1]
                                                 ).then_inc(sem("diag"), 1)
                act.wait_ge(sem("peer_done"), t + 1)
                final = xn2[:, t % 2, :]
                copy(final[:, 0:512], ps[4 + 2 * (t % 2)][:], "fin_sq", ACT.Square, accum_out=ss[:, 12:13])
                copy(final[:, 512:], ps[5 + 2 * (t % 2)][:], "fin_sq", ACT.Square, accum_out=ss[:, 13:14])

            score_keys(0)
            softmax_exp(0)
            for t in range(NT):
                if t + 1 < NT:
                    score_keys(t + 1)
                experts(t)
                if t + 1 < NT:
                    softmax_exp(t + 1)

        @block.vector
        def _(dve):
            n = {}
            v = nc.vector

            def go(ins, name="dve_step"):
                link(dve, ins, name, n)

            def rms(o, i, width, name):
                m, t = sq[:, 0:1], sq[:, 1:2]
                go(v.tensor_scalar(m, i, 1.0 / width, EPS, ALU.mult, ALU.add))
                go(v.tensor_scalar(t.bitcast(I32), m.bitcast(I32), 1, None, ALU.logical_shift_right))
                go(v.tensor_scalar(o.bitcast(I32), t.bitcast(I32), -1.0, float(0x5f3759df), ALU.mult, ALU.add))
                for step in range(3):
                    go(v.scalar_tensor_tensor(t, o, m, o, ALU.mult, ALU.mult))
                    go(v.tensor_scalar(t, t, -0.5, 1.5, ALU.mult, ALU.add))
                    go(v.tensor_tensor(o, o, t, ALU.mult), name if step == 2 else "dve_step")

            v.memset(actv[:, 0], 0.0).then_inc(sem("dots"), 8)
            v.memset(actv[:, 1], 0.0).then_inc(sem("up_free"), 8)
            go(v.memset(rb[N_BUCKETS:N_BUCKETS + 1, :], 1.0), "rb_ones")
            for t in range(NT):
                dve.wait_ge(sem("sq_x"), t + 1)
                rms(ss[:, 8 + t:9 + t], ss[:, t:t + 1], D, "dve_step")
                if t >= 2:
                    dve.wait_ge(sem("xT_ps"), t - 1)
                go(v.tensor_scalar(xn[:, t % 2, :], h[:, t, :], ss[:, 8 + t:9 + t], None, ALU.mult), "xn_ready")
                dve.wait_ge(sem("xT_ps"), t + 1)
                dve.wait_ge(sem("wmix_in"), 16)
                for b in range(2):
                    go(v.tensor_tensor(xnT[:, 4 * b:4 * b + 4, t * P:(t + 1) * P],
                                       ps[2 * (t % 2) + b][:].rearrange("p (k t) -> p k t", k=4),
                                       wmix[:, 4 * b:4 * b + 4].unsqueeze(2).to_broadcast([P, 4, P]), ALU.mult), "xT_sb")
            dve.wait_ge(sem("conv_in"), 32)
            dve.wait_ge(sem("const"), LOADS["const"])
            dve.wait_ge(sem("line_out"), 16)
            for j in range(NXB):
                dve.wait_ge(sem("proj_out"), j + 1)
                go(v.tensor_scalar(xconv[:, j, :], xraw[:, j, 0:SEQ], cw[:, 0, j:j + 1], None, ALU.mult))
                for k in range(1, CONV):
                    go(v.scalar_tensor_tensor(xconv[:, j, :], xraw[:, j, k:k + SEQ], cw[:, k, j:j + 1], xconv[:, j, :],
                                              ALU.mult, ALU.add), "conv_done" if k == CONV - 1 else "dve_step")
            dve.wait_ge(sem("rows_in"), 80)
            dve.wait_ge(sem("proj_out"), NBLK + 1)
            u, ab, ex, s, s2, acc, dt, a = (dtv[:, i, :] for i in range(8))
            br = lambda i: hrow[:, i, :].unsqueeze(1).to_broadcast([P, NT, SH])
            as4 = lambda z: z.rearrange("p (t h) -> p t h", t=NT)
            go(v.tensor_tensor(as4(u), as4(u), br(0), ALU.add))
            go(v.tensor_scalar(s, u, -1.0, None, ALU.mult))
            go(v.tensor_tensor(ab, u, s, ALU.max), "dt_abs")
            dve.wait_ge(sem("dt_exp"), 2)
            go(v.tensor_scalar(s, ex, 2.0, None, ALU.add))
            go(v.reciprocal(s2, s))
            go(v.tensor_tensor(s, ex, s2, ALU.mult))
            go(v.tensor_tensor(s2, s, s, ALU.mult))
            TERMS = 9
            go(v.memset(acc, 1.0 / (2 * TERMS - 1)))
            for k in range(TERMS - 2, -1, -1):
                go(v.tensor_tensor(acc, acc, s2, ALU.mult))
                go(v.tensor_scalar(acc, acc, 1.0 / (2 * k + 1), None, ALU.add))
            go(v.scalar_tensor_tensor(acc, acc, 2.0, s, ALU.mult, ALU.mult))
            go(v.scalar_tensor_tensor(dt, u, 0.0, acc, ALU.max, ALU.add))
            go(v.tensor_tensor(as4(a), as4(dt), br(1), ALU.mult))
            go(v.tensor_scalar(a, a, -1.0, None, ALU.mult), "a_ready")
            dve.wait_ge(sem("conv_act"), NXB)
            dve.wait_ge(sem("bias_in"), 16)

            def heads(z):
                return z.rearrange("p (h c) -> p h c", h=SH)

            def per_head(z):
                return z.unsqueeze(2).to_broadcast([P, SH, SP])

            for c in range(NT):
                dtc = dt[:, c * SH:(c + 1) * SH]
                dve.wait_ge(sem("decays"), 3 * c + 2)
                go(v.tensor_tensor(sm[:, 4, :], ps[7][:, 8:16], sm[:, 0, :], ALU.subtract), "to_end")
                dve.wait_ge(sem("nat_sb"), 3 * c + 3)
                dve.wait_ge(sem("decays"), 3 * c + 3)
                go(v.tensor_tensor(heads(xdt), heads(xs), per_head(dtc), ALU.mult), "xdt")
                go(v.tensor_tensor(heads(xend), heads(xdt), per_head(sm[:, 3, :]), ALU.mult), "xend")
                for g in range(SG):
                    dve.wait_ge(sem("seg_ps"), SG * c + g + 1)
                    go(v.tensor_tensor(decay[:, g].rearrange("p (r l) -> p r l", r=SR),
                                       ps[2 + g][:].rearrange("p (r l) -> p r l", r=SR),
                                       sm[:, 0, SR * g:SR * g + SR].unsqueeze(2).to_broadcast([P, SR, P]),
                                       ALU.subtract), "seg_sb")
                for g in range(SG):
                    dve.wait_ge(sem("seg_exp"), SG * c + g + 1)
                    dg = decay[:, g].rearrange("p (r l) -> p r l", r=SR)
                    go(v.tensor_tensor(dg, dg, cbT[:, g * P:(g + 1) * P].unsqueeze(1).to_broadcast([P, SR, P]),
                                       ALU.mult), "lm_ready")
                dve.wait_ge(sem("y_ps"), c + 1)
                go(v.tensor_tensor(heads(y1), heads(xs), per_head(hrow[:, 2, :]), ALU.mult))
                go(v.tensor_tensor(y1, y1, ps[4][:], ALU.add))
                if c:
                    go(v.tensor_tensor(heads(y2), heads(ps[5][:]), per_head(sm[:, 1, :]), ALU.mult))
                    go(v.tensor_tensor(y1, y1, y2, ALU.add))
                    go(v.tensor_tensor(heads(state[:]), heads(state[:]), per_head(sm[:, 2, :]), ALU.mult))
                    go(v.tensor_tensor(state[:], state[:], ps[6][:], ALU.add), "state_ready")
                else:
                    go(v.tensor_copy(state[:], ps[6][:]), "state_ready")
                go(v.tensor_tensor(y1, y1, zs[:, c, :], ALU.mult))
                go(v.tensor_tensor_reduce(y2, y1, y1, 1.0, 0.0, ALU.mult, ALU.add, sm[:, 5, 0:1]))
                rms(sm[:, 5, 1:2], sm[:, 5, 0:1], 512, "dve_step")
                go(v.scalar_tensor_tensor(mix[:, 512:], y1, sm[:, 5, 1:2], wn[:], ALU.mult, ALU.mult), "y_done")
                k0 = 0 if c else P
                dve.wait_ge(sem("score_ps"), c + 1)
                for b in range(4):
                    src = ps[b][:].rearrange("p (h k) -> p h k", h=2)
                    go(v.scalar_tensor_tensor(prob[:, 2 * b:2 * b + 2, k0:], src[:, :, k0:], float(HD) ** -0.5,
                                              bias[:, 2 * b:2 * b + 2, k0:], ALU.mult, ALU.add), "score_sb")
                go(v.tensor_reduce(sm[:, 10, :], prob[:, :, k0:], AX.X, ALU.max))
                go(v.tensor_tensor(sm[:, 10, :], sm[:, 10, :], hrow[:, 3, :], ALU.max))
                go(v.tensor_tensor(sm[:, 7, :], hrow[:, 3, :], sm[:, 10, :], ALU.subtract))
                go(v.tensor_scalar(sm[:, 6, :], sm[:, 10, :], -1.0, None, ALU.mult), "neg_max")
                dve.wait_ge(sem("prob_exp"), 9 * c + 9)
                go(v.tensor_tensor(sm[:, 11, :], sm[:, 8, :], sm[:, 9, :], ALU.add))
                go(v.reciprocal(sm[:, 11, :], sm[:, 11, :]))
                dve.wait_ge(sem("pv_ps"), c + 1)
                go(v.tensor_tensor(heads(mix[:, 0:512]), heads(ps[0][:]), per_head(sm[:, 11, :]), ALU.mult), "mix_ready")
                dve.wait_ge(sem("wo_ps"), c + 1)
                go(v.tensor_tensor(h[:, c, 0:512], h[:, c, 0:512], ps[3][:], ALU.add))
                go(v.tensor_tensor(h[:, c, 512:], h[:, c, 512:], ps[4][:], ALU.add), "h_mixed")

            def norm_ffn_tile(t):
                dve.wait_ge(sem("wffn_in"), 32)
                dve.wait_ge(sem("sq_h"), t + 1)
                rms(ss[:, 8 + t:9 + t], ss[:, 4 + t:5 + t], D, "dve_step")
                if t >= 2:
                    dve.wait_ge(sem(f"stored{t - 2}"), 16)
                go(v.scalar_tensor_tensor(xn2[:, t % 2, :], h[:, t, :], ss[:, 8 + t:9 + t], w_ffn, ALU.mult, ALU.mult),
                   "xn2_ready")
                if t == 0:
                    go(v.tensor_copy(iota16, iota16i[:]))

            def top16(values, vals, where):
                v.max(vals[:, 0:8], values)
                v.drain()
                v.max_index(where[:, 0:8], vals[:, 0:8], values)
                v.drain()
                v.match_replace(values, vals[:, 0:8], values, LOWEST)
                v.drain()
                v.max(vals[:, 8:16], values)
                v.drain()
                v.max_index(where[:, 8:16], vals[:, 8:16], values)

            def search_halves(r):
                v.drain()
                v.tensor_copy(pair.rearrange("p s n -> p (s n)"),
                              score.rearrange("p j n -> p (j n)")[:, bass.ds(r * 2 * NK, 2 * NK)])
                v.drain()
                for s_ in range(2):
                    top16(pair[:, s_, :], pval[:, s_, :], pidx[:, s_, :])
                v.drain()
                v.tensor_copy(pidf, pidx)

            def search_sums(r, b):
                v.tensor_tensor(sums.rearrange("p (a b) -> p a b", a=TOPK),
                                pval[:, 0, :].unsqueeze(2).to_broadcast([P, TOPK, TOPK]),
                                pval[:, 1, :].unsqueeze(1).to_broadcast([P, TOPK, TOPK]), ALU.add)
                v.drain()
                top16(sums, tval, tpos)
                v.drain()
                v.tensor_scalar(digit[:, 0, :], tpos, 4, None, ALU.logical_shift_right)
                v.tensor_scalar(digit[:, 1, :], tpos, 15, None, ALU.bitwise_and)
                v.drain()
                v.tensor_copy(digf, digit)
                v.drain()
                v.tensor_tensor(hit, digf.unsqueeze(3).to_broadcast([P, 2, TOPK, TOPK]),
                                iota16.unsqueeze(1).unsqueeze(1).to_broadcast([P, 2, TOPK, TOPK]), ALU.is_equal)
                v.drain()
                v.tensor_tensor(hit, hit, pidf.unsqueeze(2).to_broadcast([P, 2, TOPK, TOPK]), ALU.mult)
                v.drain()
                v.tensor_reduce(part, hit, AX.X, ALU.add)
                v.drain()
                v.scalar_tensor_tensor(pick, part[:, 0, :], float(NK), part[:, 1, :], ALU.mult, ALU.add)
                v.drain()
                v.tensor_copy(idx[:, b, bass.ds(r * TOPK, TOPK)], pick)
                v.tensor_copy(top.rearrange("p h k -> p (h k)")[:, bass.ds(r * TOPK, TOPK)], tval)

            def softmax(t):
                hk = lambda z: z.rearrange("p (h k) -> p h k", h=PH)
                v.drain()
                go(v.tensor_tensor(hk(eg), top, top[:, :, 0:1].to_broadcast([P, PH, TOPK]), ALU.subtract), "gate_in")
                dve.wait_ge(sem("gate_exp"), t + 1)
                go(v.tensor_reduce(gsum[:, 0, :], hk(eg), AX.X, ALU.add))
                go(v.reciprocal(gsum[:, 1, :], gsum[:, 0, :]))
                go(v.tensor_tensor(hk(gate[:, t % 2, :]), hk(eg),
                                   gsum[:, 1, :].unsqueeze(2).to_broadcast([P, PH, TOPK]), ALU.mult), "routed")

            def experts(t):
                if t + 1 < NT:
                    dve.wait_ge(sem("s_sb"), 4 * (t + 2))
                with dve.Fori(0, SLOTS // GROUP // 2) as r:
                    for half in range(2):
                        g0 = t * (SLOTS // GROUP) + half
                        for i in range(GROUP):
                            dve.wait_ge(sem(f"down{i}"), 16 * (g0 + 2 * r) + 16)
                            v.tensor_tensor_reduce(down[:, i, :], down[:, i, :], xn2[:, t % 2, :], 1.0, 0.0,
                                                   ALU.mult, ALU.add, pre[:, half, i:i + 1]).then_inc(sem("dots"), 1)
                        dve.wait_ge(sem("gelu"), g0 + 2 * r + 1)
                        dve.wait_ge(sem("gnow_ready"), g0 + 2 * r + 1)
                        v.tensor_tensor(actv[:, half], gel[:, half], gnow[:, half], ALU.mult
                                        ).then_inc(sem("act_ready"), 1)
                        if t + 1 < NT:
                            if half == 0:
                                search_halves(r)
                            else:
                                search_sums(r, (t + 1) % 2)

            def finish(t):
                final = xn2[:, t % 2, :]
                acc = ps[4 + 2 * (t % 2)], ps[5 + 2 * (t % 2)]
                dve.wait_ge(sem("fin_sq"), 2 * t + 2)
                go(v.tensor_tensor(ss[:, 14:15], ss[:, 12:13], ss[:, 13:14], ALU.add))
                rms(ss[:, 15:16], ss[:, 14:15], D, "dve_step")
                go(v.scalar_tensor_tensor(final[:, 0:512], acc[0][:], ss[:, 15:16], w_fin[:, 0:512], ALU.mult, ALU.mult))
                go(v.scalar_tensor_tensor(final[:, 512:], acc[1][:], ss[:, 15:16], w_fin[:, 512:], ALU.mult, ALU.mult),
                   "final_ready")

            norm_ffn_tile(0)
            dve.wait_ge(sem("s_sb"), 4)
            with dve.Fori(0, PH) as r:
                search_halves(r)
                v.drain()
                search_sums(r, 0)
            softmax(0)
            for t in range(NT):
                if t + 1 < NT:
                    norm_ffn_tile(t + 1)
                experts(t)
                if t + 1 < NT:
                    softmax(t + 1)
                finish(t)

        @block.tensor
        def _(pe):
            mm = nc.tensor.matmul
            pe.wait_ge(sem("const"), LOADS["const"])
            for t in range(NT):
                pe.wait_ge(sem("xn_ready"), t + 1)
                if t >= 2:
                    pe.wait_ge(sem("xT_sb"), 2 * (t - 1))
                for k in range(KT):
                    last = nc.tensor.transpose(ps[2 * (t % 2) + k // 4][:, (k % 4) * P:(k % 4 + 1) * P],
                                               xn[:, t % 2, k * P:(k + 1) * P], ident[:])
                last.then_inc(sem("xT_ps"), 1)
            pe.wait_ge(sem("line_in"), 32)
            pe.wait_ge(sem("rb_ones"), 1)
            for hh in range(HEADS):
                if hh >= 2:
                    pe.wait_ge(sem("line_done"), hh - 1)
                mm(ps[4 + hh % 2][:, 0:LW], rb[:, hh:hh + 1].to_broadcast([N_BUCKETS + 1, P]), buckets,
                   start=True, stop=True).then_inc(sem("line_ps"), 1)
            pe.wait_ge(sem("xT_sb"), 2 * NT)
            for b in range(NBLK):
                pe.wait_ge(sem(f"ring{b % RING}"), 16 * (b // RING + 1))
                if b >= 4:
                    pe.wait_ge(sem("proj_out"), b - 3)
                w = ring[:, b % RING]
                if b < B_V:
                    for k in range(KT):
                        last = mm(ps[b % 4][:], w[:, k, :], xnT[:, k, :], start=(k == 0), stop=(k == KT - 1))
                else:
                    for t in range(NT):
                        for k in range(KT):
                            last = mm(ps[b % 4][:, t * P:(t + 1) * P], xnT[:, k, t * P:(t + 1) * P], w[:, k, :],
                                      start=(k == 0), stop=(k == KT - 1))
                last.then_inc(sem("block_used"), 1)
            pe.wait_ge(sem("wdt_in"), 16)
            pe.wait_ge(sem("proj_out"), NBLK - 3)
            for t in range(NT):
                for k in range(KT):
                    last = mm(ps[NBLK % 4][:, t * SH:(t + 1) * SH], xnT[:, k, t * P:(t + 1) * P], w_dt_sb[:, k, :],
                              start=(k == 0), stop=(k == KT - 1))
            last.then_inc(sem("block_used"), 1)

            pe.wait_ge(sem("proj_out"), NBLK + 1)
            pe.wait_ge(sem("conv_act"), NXB)
            pe.wait_ge(sem("a_ready"), 1)
            a = dtv[:, 7, :]
            for c in range(NT):
                tc = slice(c * P, (c + 1) * P)
                if c:
                    pe.wait_ge(sem("h_mixed"), c)
                ac = a[:, c * SH:(c + 1) * SH]
                mm(ps[7][:, 0:8], tri[:], ac, start=True, stop=True)
                mm(ps[7][:, 8:16], ones[:], ac, start=True, stop=True).then_inc(sem("acum_ps"), 1)
                for j in range(4):
                    nc.tensor.transpose(ps[0][:, j * P:(j + 1) * P], xconv[:, j, tc], ident[:])
                for g in range(SG):
                    nc.tensor.transpose(ps[1][:, g * P:(g + 1) * P], xconv[:, 4 + g, tc], ident[:])
                for g in range(SG):
                    last = mm(ps[1][:, (2 + g) * P:(3 + g) * P], xconv[:, 4 + g, tc], xconv[:, 6 + g, tc],
                              start=True, stop=True)
                last.then_inc(sem("nat_ps"), 1)
                for g in range(SG):
                    bank = ps[2 + g][:].rearrange("p (r l) -> p r l", r=SR)
                    mm(bank, ident[:], negm[:].unsqueeze(1).to_broadcast([P, SR, P]), start=True, stop=False,
                       skip_group_check=True)
                    for r in range(SR):
                        hh = g * SR + r
                        last = mm(bank[:, r, :], ac[:, hh:hh + 1].to_broadcast([P, P]), tri[:], start=False,
                                  stop=(r == SR - 1), skip_group_check=True)
                    last.then_inc(sem("seg_ps"), 1)
                if c:
                    pe.wait_ge(sem("state_ready"), c)
                    for g in range(SG):
                        mm(ps[5][:, g * 256:(g + 1) * 256], xconv[:, 6 + g, tc], state[:, g * 256:(g + 1) * 256],
                           start=True, stop=True)
                pe.wait_ge(sem("xend"), c + 1)
                for g in range(SG):
                    mm(ps[6][:, g * 256:(g + 1) * 256], bnat[:, g * P:(g + 1) * P], xend[:, g * 256:(g + 1) * 256],
                       start=True, stop=True)
                pe.wait_ge(sem("lm_ready"), SG * (c + 1))
                for hh in range(SH):
                    last = mm(ps[4][:, hh * SP:(hh + 1) * SP], decay[:, hh // SR, (hh % SR) * P:(hh % SR + 1) * P],
                              xdt[:, hh * SP:(hh + 1) * SP], start=True, stop=True)
                last.then_inc(sem("y_ps"), 1)
                k0 = 0 if c else P
                for hh in range(HEADS):
                    half = slice(HD * (hh // 4), HD * (hh // 4) + HD)
                    last = mm(ps[hh // 2][:, (hh % 2) * 256 + k0:(hh % 2) * 256 + 256],
                              qkT[half, 1 + hh % 4, tc], qkT[half, 0, c * P - P + k0:(c + 1) * P], start=True, stop=True)
                last.then_inc(sem("score_ps"), 1)
                pe.wait_ge(sem("prob_exp"), 9 * c + 9)
                pe.wait_ge(sem("y_done"), c + 1)
                for hh in range(HEADS):
                    for kb in range(0 if c else 1, 2):
                        last = nc.tensor.transpose(ps[4 + hh // 2][:, ((hh % 2) * 2 + kb) * P:((hh % 2) * 2 + kb + 1) * P],
                                                   prob[:, hh, kb * P:(kb + 1) * P], ident[:])
                last.then_inc(sem("pt_ps"), 1)
                pe.wait_ge(sem("pt_sb"), 4 * c + 4)
                for hh in range(HEADS):
                    for kb in range(0 if c else 1, 2):
                        i = (hh % 2) * 2 + kb
                        last = mm(ps[0][:, hh * HD:(hh + 1) * HD], probT[:, hh // 2, i * P:(i + 1) * P],
                                  v_sb[:, c - 1 + kb, (hh // 4) * HD:(hh // 4 + 1) * HD], start=(kb == 0 or c == 0),
                                  stop=(kb == 1))
                last.then_inc(sem("pv_ps"), 1)
                pe.wait_ge(sem("mix_ready"), c + 1)
                for k in range(KT):
                    last = nc.tensor.transpose(ps[1 + k // 4][:, (k % 4) * P:(k % 4 + 1) * P], mix[:, k * P:(k + 1) * P],
                                               ident[:])
                last.then_inc(sem("mixT_ps"), 1)
                pe.wait_ge(sem("mixT_sb"), 2 * c + 2)
                pe.wait_ge(sem("wo_in"), 16)
                for b in range(2):
                    for k in range(KT):
                        last = mm(ps[3 + b][:], mixT[:, k, :], wo[:, k, b * 512:(b + 1) * 512], start=(k == 0),
                                  stop=(k == KT - 1))
                last.then_inc(sem("wo_ps"), 1)

            def score_keys(t):
                pe.wait_ge(sem("xn2_ready"), t + 1)
                for k in range(KT):
                    last = nc.tensor.transpose(ps[k // 4][:, (k % 4) * P:(k % 4 + 1) * P],
                                               xn2[:, t % 2, k * P:(k + 1) * P], ident[:])
                last.then_inc(sem("xn2T_ps"), 1)
                pe.wait_ge(sem("xn2T_sb"), 2 * t + 2)
                pe.wait_ge(sem("wq_in"), 48)
                for b in range(4):
                    if b >= 2:
                        pe.wait_ge(sem("q_sb"), 4 * t + b - 1)
                    for j in range(4):
                        for k in range(KT):
                            col = (4 * b + j) * P
                            last = mm(ps[2 + b % 2][:, j * P:(j + 1) * P], wq[:, k, col:col + P], xn2T[:, k, :],
                                      start=(k == 0), stop=(k == KT - 1))
                    last.then_inc(sem("q_ps"), 1)
                for b in range(4):
                    pe.wait_ge(sem("q_sb"), 4 * t + b + 1)
                    if b >= 2:
                        pe.wait_ge(sem("s_sb"), 4 * t + b - 1)
                    for j in range(4):
                        last = mm(ps[b % 2][:, j * P:(j + 1) * P], qT[:, 4 * b + j, :], keysT[:, j % 2, :],
                                  start=True, stop=True)
                    last.then_inc(sem("s_ps"), 1)

            def experts(t):
                acc = ps[4 + 2 * (t % 2)], ps[5 + 2 * (t % 2)]
                if t >= 2:
                    pe.wait_ge(sem("final_ready"), t - 1)
                elif t == 0:
                    pe.wait_ge(sem("h_mixed"), NT)
                for b in range(2):
                    mm(acc[b][:], ident[:], h[:, t, b * 512:(b + 1) * 512], start=True, stop=False,
                       skip_group_check=True)
                with pe.Fori(0, SLOTS // GROUP // 2) as r:
                    for half in range(2):
                        g0 = t * (SLOTS // GROUP) + half
                        for i in range(GROUP):
                            pe.wait_ge(sem("diag"), 8 * (g0 + 2 * r) + i + 1)
                            pe.wait_ge(sem(f"up{i}"), 16 * (g0 + 2 * r) + 16)
                            mm(acc[0][:], diag[:, i, :], up[:, i, 0:512], start=False, stop=False,
                               skip_group_check=True)
                            mm(acc[1][:], diag[:, i, :], up[:, i, 512:], start=False, stop=False,
                               skip_group_check=True).then_inc(sem("up_free"), 1)
                pe.wait_ge(sem("up_free"), 8 + SLOTS * (t + 1))
                pe.nop(nofuse=True).then_inc(sem("peer_done"), 1)

            score_keys(0)
            for t in range(NT):
                if t + 1 < NT:
                    score_keys(t + 1)
                experts(t)


def bucket_lines():
    dist = P + P - 1 - np.arange(LW)
    n = np.maximum(dist, 0)
    exact = N_BUCKETS // 2
    nf = np.maximum(n, 1).astype(np.float32)
    large = exact + (np.log(nf / np.float32(exact)) / np.float32(math.log(MAX_DISTANCE / exact))
                     * np.float32(N_BUCKETS - exact)).astype(np.int32)
    large = np.minimum(large, N_BUCKETS - 1)
    which = np.where(n < exact, n, large)
    ok = (dist >= 0) & (dist < WINDOW)
    lines = np.zeros((N_BUCKETS + 1, LW), np.float32)
    lines[which[ok], np.nonzero(ok)[0]] = 1.0
    lines[N_BUCKETS, ~ok] = NEG
    return lines


def kernel(**inputs):
    import numpy as _np
    import concourse.bacc as _bacc
    from concourse import mybir as _mybir
    from concourse.bass_utils import run_bass_kernel_spmd as _run

    g = {k: _np.asarray(a) for k, a in inputs.items()}
    w = g["w_in"][0]
    kv = HEADS * HD
    off_v, off_z = kv + KV_HEADS * HD, kv + 2 * KV_HEADS * HD
    off_x = off_z + SH * SP
    off_dt = off_x + XBC
    cols = [_np.arange(off_x + j * P, off_x + (j + 1) * P) for j in range(NXB)]
    cols += [_np.arange(kv, off_v)]
    cols += [_np.concatenate([_np.arange(j * HD, (j + 1) * HD), _np.arange((4 + j) * HD, (5 + j) * HD)]) for j in range(4)]
    cols += [_np.arange(off_v, off_z)]
    cols += [_np.arange(off_z + j * P, off_z + (j + 1) * P) for j in range(4)]

    def by_rows(m):
        return _np.ascontiguousarray(m.reshape(KT, P, m.shape[1]).transpose(1, 0, 2).reshape(P, -1))

    host = {
        "x": g["x"], "w_in_blocks": _np.stack([by_rows(w[:, c]) for c in cols]), "w_dt": by_rows(w[:, off_dt:]),
        "norm_mix": g["norm_mix"][0].reshape(KT, P).T,
        "conv_w": g["conv_w"][0].reshape(CONV, NXB, P).transpose(2, 0, 1), "conv_b": g["conv_b"][0].reshape(NXB, P).T,
        "dt_bias": g["dt_bias"],
        "a_log": g["a_log"], "d_skip": g["d_skip"], "ssd_norm_w": g["ssd_norm_w"], "sinks": g["attn_sinks"],
        "w_out": g["w_out"][0], "rel_bias": g["rel_bias"], "bucket_line": bucket_lines(), "norm_ffn": g["norm_ffn"],
        "w_query": g["w_query"][0], "keys1_t": g["sub_keys1"][0].T, "keys2_t": g["sub_keys2"][0].T,
        "expert_down": g["expert_down"][0], "expert_up": g["expert_up"][0], "norm_final": g["norm_final"][None],
    }
    nc = _bacc.Bacc("TRN2", target_bir_lowering=False, num_devices=1)
    arrays, args = {}, []
    for name, a in host.items():
        a = _np.ascontiguousarray(a)
        arrays[f"in_{name}_dram"] = a
        args.append(nc.dram_tensor(f"in_{name}_dram", a.shape, _mybir.dt.from_np(a.dtype), kind="ExternalInput").ap())
    out = nc.dram_tensor("out_0_dram", (1, SEQ, D), F32, kind="ExternalOutput").ap()
    layer(nc, *args, out)
    r = _run(nc, [arrays], core_ids=[0])
    return r.results[0]["out_0_dram"]
```

```python
import math
from contextlib import ExitStack

import numpy as np

import concourse.bass as bass
from concourse import mybir

ALU = mybir.AluOpType
ACT = mybir.ActivationFunctionType
AX = mybir.AxisListType
F32 = mybir.dt.float32
I32 = mybir.dt.int32
U32 = mybir.dt.uint32

P = 128
D = 1024
KT = D // P
SEQ = 512
NT = SEQ // P
HEADS, KV_HEADS, HD = 8, 2, 64
WINDOW = 128
N_BUCKETS, MAX_DISTANCE = 32, 128
SH, SP, SN, SG = 8, 64, 128, 2
SR = SH // SG
CONV = 4
XBC = SH * SP + 2 * SG * SN
NXB = XBC // P
PH, NK, TOPK = 8, 128, 16
SLOTS = PH * TOPK
GROUP = 8
EPS = 1e-6
NEG = -1e30
LOWEST = -3.0e38
LW = 3 * P
NBLK = NXB + 5 + 4 + 1
RING = 5
B_K, B_Q, B_Z, B_V = NXB, NXB + 1, NXB + 5, NXB + 9
DT = -1
STEPS = [*range(NXB), DT, *range(NXB, NBLK)]
BY_DVE = STEPS.index(B_Z)
LATE = len(STEPS) - 3


def step_bank(n_step):
    return n_step % 4 if n_step < LATE else (5, 5, 6)[n_step - LATE]


def layer(nc, x, w_in_blocks, w_dt, norm_mix, conv_w, conv_b, dt_bias, a_log, d_skip, ssd_norm_w, sinks, w_out,
          rel_bias, bucket_line, norm_ffn, w_query, keys1_t, keys2_t, expert_down, expert_up, norm_final, out):
    line_dram = nc.dram_tensor("line_scratch", (P, HEADS * LW), F32, kind="Internal").ap()
    with ExitStack() as ctx:
        def sb(name, shape, dt=F32):
            return ctx.enter_context(nc.sbuf_tensor(name, shape, dt))

        SEMS = {}

        def sem(name):
            if name not in SEMS:
                SEMS[name] = ctx.enter_context(nc.semaphore(name))
            return SEMS[name]

        arena = sb("arena", [P, 24 * D])
        arena2 = sb("arena2", [P, 6 * D])
        wq = sb("wq", [P, KT, PH * 2 * P])
        h = sb("h", [P, NT, D])

        def slot(i, n=1, of=arena):
            return of[:, i * D:(i + n) * D]

        xnT = slot(0, 4).rearrange("p (k t) -> p k t", k=KT)
        ring = slot(4, RING).rearrange("p (s k c) -> p s k c", s=RING, k=KT)
        PAD = CONV - 1
        xraw = arena[:, 9 * D:9 * D + NXB * (SEQ + PAD)].rearrange("p (j t) -> p j t", j=NXB)
        xconv = slot(14, 4).rearrange("p (j t) -> p j t", j=NXB)
        zs = slot(18, 2).rearrange("p (t c) -> p t c", t=NT)
        qkT = arena[:, 20 * D:20 * D + 5 * SEQ].rearrange("p (j t) -> p j t", j=5)
        v_sb = arena[:, 23 * D:23 * D + NT * P].rearrange("p (t c) -> p t c", t=NT)
        wo = slot(0, 8).rearrange("p (k c) -> p k c", k=KT)
        bias = slot(0, 2, arena2).rearrange("p (h k) -> p h k", h=HEADS)
        prob = slot(2, 2, arena2).rearrange("p (h k) -> p h k", h=HEADS)
        probT = slot(4, 2, arena2).rearrange("p (b c) -> p b c", b=4)
        r_diag = slot(4, 1, arena2)[:, 0:SEQ].rearrange("p (t c) -> p t c", t=NT)
        r_all = slot(4, 1, arena2)[:, SEQ:2 * SEQ]
        line = arena[0:HEADS, 14 * D:14 * D + LW]
        buckets = arena[0:N_BUCKETS + 1, 18 * D:18 * D + LW]
        xs = slot(9)[:, 0:512]
        xdt = slot(9)[:, 512:1024]
        xend = slot(10)[:, 0:512]
        bnat = slot(10)[:, 512:768]
        cbT = slot(10)[:, 768:1024]
        decay = slot(11).rearrange("p (g c) -> p g c", g=SG)
        mix = slot(12)
        mixT = [slot(17 if c == NT - 1 else 13).rearrange("p (k t) -> p k t", k=KT) for c in range(NT)]
        y1 = arena[:, 23 * D + 512:24 * D]
        y2 = arena[:, 22 * D + 512:23 * D]
        up = slot(0, 8).rearrange("p (s c) -> p s c", s=8)
        down = slot(8, 8).rearrange("p (s c) -> p s c", s=8)
        xn2 = slot(16, 2).rearrange("p (b c) -> p b c", b=2)
        xn2T = slot(18).rearrange("p (k t) -> p k t", k=KT)
        one = slot(19)
        pair = one[:, 0:256].rearrange("p (s n) -> p s n", s=2)
        sums = one[:, 256:512]
        pval = one[:, 512:544].rearrange("p (s k) -> p s k", s=2)
        pidx = one[:, 544:576].bitcast(U32).rearrange("p (s k) -> p s k", s=2)
        pidf = one[:, 576:608].rearrange("p (s k) -> p s k", s=2)
        tval = one[:, 608:624]
        tpos = one[:, 624:640].bitcast(U32)
        digit = one[:, 640:672].bitcast(U32).rearrange("p (s k) -> p s k", s=2)
        digf = one[:, 672:704].rearrange("p (s k) -> p s k", s=2)
        part = one[:, 704:736].rearrange("p (s k) -> p s k", s=2)
        pick = one[:, 736:752]
        score = slot(21, 2).rearrange("p (j n) -> p j n", j=2 * PH)
        hit = slot(23)[:, 0:512].rearrange("p (s k a) -> p s k a", s=2, k=TOPK)
        qT = slot(0, 2, arena2).rearrange("p (j t) -> p j t", j=2 * PH)
        diag = slot(2, 1, arena2).rearrange("p (s c) -> p s c", s=GROUP)
        w_ffn = slot(3, 1, arena2)
        early_w = slot(8)
        early_keys = xconv[:, 0:2, 0:P]
        w_fin = slot(4, 1, arena2)
        keep = slot(5, 1, arena2)
        idx = keep[:, 0:256].bitcast(I32).rearrange("p (b m) -> p b m", b=2)
        gate = keep[:, 256:512].rearrange("p (b m) -> p b m", b=2)
        keysT = keep[:, 512:768].rearrange("p (s n) -> p s n", s=2)

        ident = sb("ident", [P, P])
        tri = sb("tri", [P, P])
        ones = sb("ones", [P, P])
        state = sb("state", [P, 512])
        wn = sb("wn", [P, 512])
        wmix = sb("wmix", [P, KT])
        early = slot(2, 1, arena2)
        w_dt_sb = early[:, 0:64].rearrange("p (k c) -> p k c", k=KT)
        cw = early[:, 64:96].rearrange("p (w j) -> p w j", w=CONV)
        cb = early[:, 96:104]
        rb = sb("rb", [N_BUCKETS + 1, HEADS])
        hrow = sb("hrow", [P, 4, SH])
        ss = sb("ss", [P, 16])
        dtv = sb("dtv", [P, 8, NT * SH])
        sm = sb("sm", [P, 12, SH])
        wide = slot(20)
        eg = slot(23)[:, 512:528]
        tdiff = slot(23)[:, 528:544]
        gsum = slot(23)[:, 544:546]
        iota16 = keep[:, 856:872]
        iota16i = sb("iota16i", [P, TOPK], I32)
        inow = keep[:, 768:784].bitcast(I32).rearrange("p (b i) -> p b i", b=2)
        gnow, pre, gel = (keep[:, 784 + 16 * i:800 + 16 * i].rearrange("p (b i) -> p b i", b=2) for i in range(3))
        sq = sb("sq", [P, 8])
        actv = sb("actv", [P, 2, GROUP])

        ps = [ctx.enter_context(nc.psum_tensor(f"ps{i}", [P, 512], F32)) for i in range(8)]

        PT = (4, 7, 0, 1)
        PT_ORDER = [(0, 1, 2, 3)] * (NT - 1) + [(0, 1, 3, 2)]

        block = ctx.enter_context(nc.Block())

        def link(eng, ins, name, count):
            count[name] = count.get(name, 0) + 1
            ins.then_inc(sem(name), 1)
            eng.wait_ge(sem(name), count[name])

        LOADS = {}

        def tile_steps(eng, t, iteration, middle=lambda t, n: None):
            if t == 0:
                for r in range(3):
                    iteration(t, r)
                    if r < 2:
                        middle(0, r)
            else:
                with eng.Fori(0, 3) as r:
                    iteration(t, r)
            middle(t + 1, 0)
            iteration(t, 3)
            middle(t + 1, 1)
            with eng.Fori(4, 6) as r:
                iteration(t, r)
            middle(t + 1, 2)
            iteration(t, 6)
            iteration(t, 7)


        @block.sync
        def _(sp):
            for t in range(NT):
                sp.dma_start(h[:, t, :], x[0, t * P:(t + 1) * P, :]).then_inc(sem(f"x_in{t}"), 16)
                if t == 0:
                    sp.dma_start(buckets, bucket_line).then_inc(sem("line_in"), 16)
                    sp.dma_start(rb[0:N_BUCKETS, :], rel_bias).then_inc(sem("line_in"), 16)
                    sp.dma_start(wmix[:], norm_mix).then_inc(sem("wmix_in"), 16)
            for b in range(NBLK):
                if b >= RING:
                    sp.wait_ge(sem("block_used"), b - RING + 1)
                sp.dma_start(ring[:, b % RING], w_in_blocks[b].rearrange("p (k c) -> p k c", k=KT)
                             ).then_inc(sem(f"ring{b % RING}"), 16)
                if b == 2:
                    sp.dma_start(cw, conv_w).then_inc(sem("conv_in"), 16)
                    sp.dma_start(cb, conv_b).then_inc(sem("conv_in"), 16)
                if b == 3:
                    sp.dma_start(w_dt_sb, w_dt.rearrange("p (k c) -> p k c", k=KT)).then_inc(sem("wdt_in"), 16)
                    for i, row in enumerate((dt_bias, a_log, d_skip, sinks)):
                        sp.dma_start(hrow[:, i, :], row.to_broadcast([P, SH])).then_inc(sem("rows_in"), 16)
                    sp.dma_start(wn[:], ssd_norm_w.to_broadcast([P, 512])).then_inc(sem("rows_in"), 16)
                if b == 5:
                    sp.wait_ge(sem("line_done"), 1)
                    rows = bass.AP(line_dram.tensor, 0, [[LW, HEADS], [HEADS * LW, P], [1, LW]])
                    sp.dma_start(rows, line.unsqueeze(1).to_broadcast([HEADS, P, LW])).then_inc(sem("line_out"), 16)
                    sp.wait_ge(sem("line_out"), 16)
                    skew = bass.AP(line_dram.tensor, P - 1, [[HEADS * LW - 1, P], [LW, HEADS], [1, 2 * P]])
                    sp.dma_start(bias, skew).then_inc(sem("bias_in"), 16)
            sp.wait_ge(sem("block_used"), NBLK)
            sp.dma_start(wo, w_out.rearrange("(k p) c -> p k c", p=P)).then_inc(sem("wo_in"), 16)
            sp.dma_start(wq[:], w_query.rearrange("(k p) c -> p k c", p=P)).then_inc(sem("wq_in"), 16)
            sp.dma_start(early_w, norm_ffn.to_broadcast([P, D])).then_inc(sem("early_w_in"), 16)
            sp.wait_ge(sem("pv_ps"), 1)
            sp.dma_start(early_keys[:, 0, :], keys1_t).then_inc(sem("early_keys_in"), 16)
            sp.dma_start(early_keys[:, 1, :], keys2_t).then_inc(sem("early_keys_in"), 16)
            sp.wait_ge(sem("pv_ps"), NT)
            sp.dma_start(keysT[:, 0, :], keys1_t).then_inc(sem("wq_in"), 16)
            sp.dma_start(keysT[:, 1, :], keys2_t).then_inc(sem("wq_in"), 16)
            sp.dma_start(w_ffn, norm_ffn.to_broadcast([P, D])).then_inc(sem("wffn_in"), 16)
            sp.dma_start(w_fin, norm_final.to_broadcast([P, D])).then_inc(sem("wffn_in"), 16)
            for t in range(NT):
                sp.wait_ge(sem("final_ready"), t + 1)
                sp.dma_start(out[0, t * P:(t + 1) * P, :], xn2[:, t % 2, :]).then_inc(sem(f"stored{t}"), 16)
            for t in range(NT):
                sp.wait_ge(sem(f"stored{t}"), 16)

        @block.gpsimd
        def _(gp):
            n = {}
            link(gp, gp.memset(ones[:], 1.0), "const", n)
            link(gp, gp.affine_select(out=ident[:], in_=ones[:], compare_op=ALU.is_equal, fill=0.0, base=0,
                                      pattern=[[-1, P]], channel_multiplier=1), "const", n)
            link(gp, gp.affine_select(out=tri[:], in_=ones[:], compare_op=ALU.is_ge, fill=0.0, base=0,
                                      pattern=[[1, P]], channel_multiplier=-1), "const", n)
            link(gp, gp.iota(iota16i[:], pattern=[[1, TOPK]], base=0, channel_multiplier=0), "const", n)
            for j in range(NXB):
                link(gp, gp.memset(xraw[:, j, 0:PAD], 0.0), "const", n)
            LOADS["const"] = n["const"]

            def gather(t, r):
                gp.wait_ge(sem("routed"), t * PH + r + 1)
                for half in range(2):
                    g = t * (SLOTS // GROUP) + 2 * r + half
                    part = bass.ds((2 * r + half) * GROUP, GROUP)
                    if half == 0:
                        gp.wait_ge(sem("up_free"), 8 * g + 1)
                    gp.tensor_copy(inow[:, half], idx[:, t % 2, part]).then_inc(sem("inow_ready"), 1)
                    gp.wait_ge(sem("inow_ready"), g + 1)
                    for i in range(GROUP):
                        gp.wait_ge(sem("dots"), 8 * g + i + 1)
                        gp.nop(nofuse=True)
                        gp.indirect_dma_start(down[:, i, :], None, expert_down,
                                              bass.IndirectOffsetOnAxis(ap=inow[:, half, i:i + 1], axis=0)
                                              ).then_inc(sem(f"down{i}"), 16)
                    if half == 0:
                        gp.wait_ge(sem("gated"), t * PH + r + 1)
                        if t == 0:
                            gp.wait_ge(sem("wo_ps"), NT)
                    gp.tensor_copy(gnow[:, half], gate[:, t % 2, part]).then_inc(sem("gnow_ready"), 1)
                    for i in range(GROUP):
                        gp.wait_ge(sem("up_free"), 8 * g + i + 1)
                        gp.nop(nofuse=True)
                        gp.indirect_dma_start(up[:, i, :], None, expert_up,
                                              bass.IndirectOffsetOnAxis(ap=inow[:, half, i:i + 1], axis=0)
                                              ).then_inc(sem(f"up{i}"), 16)

            gp.wait_ge(sem("mixT_ps"), NT)
            for t in range(NT):
                with gp.Fori(0, PH) as r:
                    gather(t, r)

        @block.scalar
        def _(act):
            n = {}

            def copy(o, i, name="act_step", func=ACT.Copy, **kw):
                link(act, nc.scalar.activation(o, i, func, **kw), name, n)

            for t in range(NT):
                act.wait_ge(sem(f"x_in{t}"), 16)
                copy(slot(19), h[:, t, :], "sq_x", ACT.Square, accum_out=ss[:, t:t + 1])
            act.wait_ge(sem("x_rms"), 1)
            act.wait_ge(sem("const"), LOADS["const"])
            for t in range(NT):
                copy(r_diag[:, t, :], ident[:], "r_diag", scale=ss[:, 8 + t:9 + t])
            act.wait_ge(sem("r_ps"), 1)
            copy(r_all, ps[5][:], "r_all")
            act.wait_ge(sem("line_ps"), 1)
            copy(line, ps[4][0:HEADS, 0:LW], "line_done")
            act.wait_ge(sem("dt_abs"), 1)
            copy(dtv[:, 2, :], dtv[:, 1, :], "dt_exp", ACT.Exp, scale=-1.0)
            copy(hrow[:, 1, :], hrow[:, 1, :], "dt_exp", ACT.Exp)
            act.wait_ge(sem("conv_in"), 32)
            for j in range(NXB):
                act.wait_ge(sem("conv_done"), j + 1)
                copy(xconv[:, j, :], xconv[:, j, :], "conv_act", ACT.Silu, bias=cb[:, j:j + 1])

            def projected(n_step):
                b = STEPS[n_step]
                act.wait_ge(sem("step_ps"), n_step + 1)
                src = ps[step_bank(n_step)]
                for t in range(NT):
                    part = src[:, t * P:(t + 1) * P]
                    if b == B_V:
                        copy(v_sb[:, t, :], part, "zv_out", scale=ss[:, 8 + t:9 + t])
                    else:
                        copy(zs[:, t, (b - B_Z) * P:(b - B_Z + 1) * P], part, "zv_out", ACT.Silu,
                             scale=ss[:, 8 + t:9 + t])

            for n_step in range(BY_DVE, LATE):
                projected(n_step)

            def transposed(t):
                act.wait_ge(sem("xn2T_ps"), t + 1)
                for b in range(2):
                    copy(xn2T[:, 4 * b:4 * b + 4, :], ps[b][:].rearrange("p (k t) -> p k t", k=4), "xn2T_sb")

            def queries(t, b):
                act.wait_ge(sem("q_ps"), 4 * t + b + 1)
                copy(qT[:, 4 * b:4 * b + 4, :], ps[2 + b % 2][:].rearrange("p (j t) -> p j t", j=4), "q_sb")

            def scores(t, b):
                act.wait_ge(sem("s_ps"), 4 * t + b + 1)
                copy(score[:, 4 * b:4 * b + 4, :], ps[b % 2][:].rearrange("p (j t) -> p j t", j=4), "s_sb")

            def chunk_start(c):
                act.wait_ge(sem("acum_ps"), c + 1)
                if c:
                    act.wait_ge(sem("y_done"), c)
                copy(sm[:, 0, :], ps[7][:, 0:8], "acum_sb")
                copy(sm[:, 1, :], ps[7][:, 0:8], "decays", ACT.Exp)
                copy(sm[:, 2, :], ps[7][:, 8:16], "decays", ACT.Exp)
                act.wait_ge(sem("nat_ps"), c + 1)
                copy(xs, ps[0][:], "nat_sb")
                act.wait_ge(sem("cb_ready"), c + 1)
                copy(bnat, ps[1][:, 0:256], "nat_sb")
                act.wait_ge(sem("to_end"), c + 1)
                copy(sm[:, 3, :], sm[:, 4, :], "decays", ACT.Exp)

            chunk_start(0)
            for c in range(NT):
                for g in range(SG):
                    act.wait_ge(sem("seg_sb"), SH * c + SR * (g + 1))
                    copy(decay[:, g], decay[:, g], "seg_exp", ACT.Exp)
                if c == 0:
                    projected(LATE)
                if c == NT - 1:
                    act.wait_ge(sem("y_ps"), NT)
                    act.wait_ge(sem("h_mixed"), 1)
                    copy(xn2[:, 1, :], h[:, 0, :], "sq_h", ACT.Square, accum_out=ss[:, 4:5])
                act.wait_ge(sem("neg_max"), c + 1)
                k0 = 0 if c else P
                for hh in range(HEADS):
                    copy(prob[:, hh, k0:], prob[:, hh, k0:], "prob_exp", ACT.Exp, bias=sm[:, 6, hh:hh + 1],
                         accum_out=sm[:, 8, hh:hh + 1])
                copy(sm[:, 9, :], sm[:, 7, :], "prob_exp", ACT.Exp)
                if c == 0:
                    projected(LATE + 1)
                    projected(LATE + 2)
                if c == NT - 1:
                    transposed(0)
                for n_bank, b in enumerate(PT_ORDER[c]):
                    if c == NT - 1 and n_bank == 2:
                        queries(0, 0)
                    if c == NT - 1 and n_bank == 3:
                        scores(0, 0)
                    act.wait_ge(sem("pt_ps"), 4 * c + n_bank + 1)
                    if c:
                        copy(probT[:, b, :], ps[PT[b]][:], "pt_sb")
                    else:
                        half = ps[PT[b]][:].rearrange("p (i q) -> p i q", i=4)[:, 1::2, :]
                        copy(probT[:, b, :].rearrange("p (i q) -> p i q", i=4)[:, 1::2, :], half, "pt_sb")
                if c < NT - 1:
                    chunk_start(c + 1)
                act.wait_ge(sem("mixT_ps"), c + 1)
                for b in range(2):
                    copy(mixT[c][:, 4 * b:4 * b + 4, :], ps[5 + b][:].rearrange("p (k t) -> p k t", k=4), "mixT_sb")

            def score_keys(t, part):
                if t == NT:
                    return
                if t == 0:
                    queries(0, 2 + part)
                    scores(0, 2 + part)
                    return
                if part == 0:
                    copy(wide, h[:, t, :], "sq_h", ACT.Square, accum_out=ss[:, 4 + t:5 + t])
                    transposed(t)
                if part < 2:
                    for b in range(2 * part, 2 * part + 2):
                        queries(t, b)
                else:
                    act.wait_ge(sem("found"), t * PH)
                    for b in range(4):
                        scores(t, b)

            def exp_gates(q):
                act.wait_ge(sem("found"), q + 1)
                nc.scalar.activation(eg, tdiff, ACT.Exp, accum_out=gsum[:, 0:1]).then_inc(sem("gate_exp"), 1)

            def experts(t, r):
                q = t * PH + r
                if not (t == NT - 1 and isinstance(r, int) and r == PH - 1):
                    exp_gates(q + 1)
                for half in range(2):
                    g = 2 * q + half
                    act.wait_ge(sem("dots"), 8 * g + 16)
                    nc.scalar.activation(gel[:, half], pre[:, half], ACT.Gelu).then_inc(sem("gelu"), 1)
                    act.wait_ge(sem("act_ready"), g + 1)
                    for i in range(GROUP):
                        act.wait_ge(sem("up_free"), 8 * g + i + 1)
                        nc.scalar.activation(diag[:, i, :], ident[:], ACT.Copy, scale=actv[:, half, i:i + 1]
                                             ).then_inc(sem("diag"), 1)

            exp_gates(0)
            queries(0, 1)
            scores(0, 1)
            for t in range(NT):
                tile_steps(act, t, experts, score_keys)
                act.wait_ge(sem("peer_done"), t + 1)
                final = xn2[:, t % 2, :]
                copy(final[:, 0:512], ps[4 + 2 * (t % 2)][:], "fin_sq", ACT.Square, accum_out=ss[:, 12:13])
                copy(final[:, 512:], ps[5 + 2 * (t % 2)][:], "fin_sq", ACT.Square, accum_out=ss[:, 13:14])

        @block.vector
        def _(dve):
            n = {}
            v = nc.vector

            def go(ins, name="dve_step"):
                link(dve, ins, name, n)

            def rms(o, i, width, name):
                cols = o.shape[1]
                """o = 1 / sqrt(i / width + eps): a first guess from the exponent's bits, then three Newton steps"""
                m, t = sq[:, 0:cols], sq[:, 4:4 + cols]
                go(v.tensor_scalar(m, i, 1.0 / width, EPS, ALU.mult, ALU.add))
                go(v.tensor_scalar(t.bitcast(I32), m.bitcast(I32), 1, None, ALU.logical_shift_right))
                go(v.tensor_scalar(o.bitcast(I32), t.bitcast(I32), -1.0, float(0x5f3759df), ALU.mult, ALU.add))
                for step in range(3):
                    go(v.tensor_tensor(t, o, m, ALU.mult))
                    go(v.tensor_tensor(t, t, o, ALU.mult))
                    go(v.tensor_scalar(t, t, -0.5, 1.5, ALU.mult, ALU.add))
                    go(v.tensor_tensor(o, o, t, ALU.mult), name if step == 2 else "dve_step")

            v.memset(actv[:, 0], 0.0).then_inc(sem("dots"), 8)
            v.memset(actv[:, 1], 0.0).then_inc(sem("up_free"), 8)
            go(v.memset(rb[N_BUCKETS:N_BUCKETS + 1, :], 1.0), "rb_ones")
            dve.wait_ge(sem("wmix_in"), 16)
            for t in range(NT):
                dve.wait_ge(sem("xT_ps"), t + 1)
                for b in range(2):
                    go(v.tensor_tensor(xnT[:, 4 * b:4 * b + 4, t * P:(t + 1) * P],
                                       ps[2 * t + b][:].rearrange("p (k t) -> p k t", k=4),
                                       wmix[:, 4 * b:4 * b + 4].unsqueeze(2).to_broadcast([P, 4, P]), ALU.mult), "xT_sb")
            dve.wait_ge(sem("sq_x"), NT)
            rms(ss[:, 8:12], ss[:, 0:4], D, "x_rms")
            dve.wait_ge(sem("r_all"), 1)

            def projected(n_step, o):
                dve.wait_ge(sem("step_ps"), n_step + 1)
                go(v.tensor_tensor(o, ps[n_step % 4][:], r_all, ALU.mult), "proj_out")

            for j in range(NXB):
                projected(j, xraw[:, j, PAD:])
                if j == 0:
                    dve.wait_ge(sem("conv_in"), 32)
                    dve.wait_ge(sem("const"), LOADS["const"])
                    dve.wait_ge(sem("line_out"), 16)
                go(v.tensor_scalar(xconv[:, j, :], xraw[:, j, 0:SEQ], cw[:, 0, j:j + 1], None, ALU.mult))
                for k in range(1, CONV):
                    go(v.scalar_tensor_tensor(xconv[:, j, :], xraw[:, j, k:k + SEQ], cw[:, k, j:j + 1], xconv[:, j, :],
                                              ALU.mult, ALU.add), "conv_done" if k == CONV - 1 else "dve_step")
            dve.wait_ge(sem("rows_in"), 80)
            dve.wait_ge(sem("step_ps"), NXB + 1)
            u, ab, ex, s, s2, acc, dt, a = (dtv[:, i, :] for i in range(8))
            br = lambda i: hrow[:, i, :].unsqueeze(1).to_broadcast([P, NT, SH])
            as4 = lambda z: z.rearrange("p (t h) -> p t h", t=NT)
            go(v.tensor_tensor(as4(u), as4(ps[NXB % 4][:, 0:NT * SH]), ss[:, 8:12].unsqueeze(2).to_broadcast([P, NT, SH]),
                               ALU.mult), "proj_out")
            go(v.tensor_tensor(as4(u), as4(u), br(0), ALU.add))
            go(v.tensor_scalar(s, u, -1.0, None, ALU.mult))
            go(v.tensor_tensor(ab, u, s, ALU.max), "dt_abs")
            dve.wait_ge(sem("dt_exp"), 2)
            go(v.tensor_scalar(s, ex, 2.0, None, ALU.add))
            go(v.reciprocal(s2, s))
            go(v.tensor_tensor(s, ex, s2, ALU.mult))
            go(v.tensor_tensor(s2, s, s, ALU.mult))
            TERMS = 9
            go(v.memset(acc, 1.0 / (2 * TERMS - 1)))
            for k in range(TERMS - 2, -1, -1):
                go(v.tensor_tensor(acc, acc, s2, ALU.mult))
                go(v.tensor_scalar(acc, acc, 1.0 / (2 * k + 1), None, ALU.add))
            go(v.scalar_tensor_tensor(acc, acc, 2.0, s, ALU.mult, ALU.mult))
            go(v.scalar_tensor_tensor(dt, u, 0.0, acc, ALU.max, ALU.add))
            go(v.tensor_tensor(as4(a), as4(dt), br(1), ALU.mult))
            go(v.tensor_scalar(a, a, -1.0, None, ALU.mult), "a_ready")
            for n_step in range(NXB + 1, BY_DVE):
                projected(n_step, qkT[:, STEPS[n_step] - B_K, :])
            dve.wait_ge(sem("conv_act"), NXB)
            dve.wait_ge(sem("bias_in"), 16)

            def heads(z):
                return z.rearrange("p (h c) -> p h c", h=SH)

            def per_head(z):
                return z.unsqueeze(2).to_broadcast([P, SH, SP])

            def add_projection(c):
                dve.wait_ge(sem("wo_ps"), c + 1)
                go(v.tensor_tensor(h[:, c, 0:512], h[:, c, 0:512], ps[5][:], ALU.add))
                go(v.tensor_tensor(h[:, c, 512:], h[:, c, 512:], ps[6][:], ALU.add), "h_mixed")

            def norm_ffn_tile(t, weights):
                dve.wait_ge(sem("sq_h"), t + 1)
                rms(ss[:, 8 + t:9 + t], ss[:, 4 + t:5 + t], D, "dve_step")
                if t >= 2:
                    dve.wait_ge(sem(f"stored{t - 2}"), 16)
                go(v.scalar_tensor_tensor(xn2[:, t % 2, :], h[:, t, :], ss[:, 8 + t:9 + t], weights, ALU.mult, ALU.mult),
                   "xn2_ready")

            def top16(values, vals, where):
                v.max(vals[:, 0:8], values)
                v.drain()
                v.max_index(where[:, 0:8], vals[:, 0:8], values)
                v.drain()
                v.match_replace(values, vals[:, 0:8], values, LOWEST)
                v.drain()
                v.max(vals[:, 8:16], values)
                v.drain()
                v.max_index(where[:, 8:16], vals[:, 8:16], values)

            def search_halves(r):
                v.drain()
                v.tensor_copy(pair.rearrange("p s n -> p (s n)"),
                              score.rearrange("p j n -> p (j n)")[:, bass.ds(r * 2 * NK, 2 * NK)])
                v.drain()
                for s_ in range(2):
                    top16(pair[:, s_, :], pval[:, s_, :], pidx[:, s_, :])
                v.drain()
                v.tensor_copy(pidf, pidx)

            for c in range(NT):
                dtc = dt[:, c * SH:(c + 1) * SH]
                dve.wait_ge(sem("decays"), 3 * c + 2)
                go(v.tensor_tensor(sm[:, 4, :], ps[7][:, 8:16], sm[:, 0, :], ALU.subtract), "to_end")
                dve.wait_ge(sem("nat_ps"), c + 1)
                go(v.tensor_tensor(cbT.rearrange("p (g l) -> p g l", g=SG),
                                   ps[1][:, 256:512].rearrange("p (g l) -> p g l", g=SG),
                                   tri[:].unsqueeze(1).to_broadcast([P, SG, P]), ALU.mult), "cb_ready")
                dve.wait_ge(sem("nat_sb"), 2 * c + 2)
                dve.wait_ge(sem("decays"), 3 * c + 3)
                go(v.tensor_tensor(heads(xdt), heads(xs), per_head(dtc), ALU.mult), "xdt")
                go(v.tensor_tensor(heads(xend), heads(xdt), per_head(sm[:, 3, :]), ALU.mult), "xend")
                v.tensor_tensor(heads(y1), heads(xs), per_head(hrow[:, 2, :]), ALU.mult).then_inc(sem("y_skip"), 1)
                for g in range(SG):
                    dve.wait_ge(sem("seg_ps"), SG * c + g + 1)
                    for r in range(SR):
                        v.tensor_scalar(decay[:, g, r * P:(r + 1) * P], ps[2 + g][:, r * P:(r + 1) * P],
                                        sm[:, 0, SR * g + r:SR * g + r + 1], 0.0, ALU.subtract, ALU.min
                                        ).then_inc(sem("seg_sb"), 1)
                for g in range(SG):
                    dve.wait_ge(sem("seg_exp"), SG * c + g + 1)
                    dg = decay[:, g].rearrange("p (r l) -> p r l", r=SR)
                    go(v.tensor_tensor(dg, dg, cbT[:, g * P:(g + 1) * P].unsqueeze(1).to_broadcast([P, SR, P]),
                                       ALU.mult), "lm_ready")
                dve.wait_ge(sem("state_ps"), c + 1)
                dve.wait_ge(sem("y_skip"), c + 1)
                if c:
                    go(v.tensor_tensor(heads(y2), heads(ps[5][:]), per_head(sm[:, 1, :]), ALU.mult), "off_read")
                    go(v.tensor_tensor(y1, y1, y2, ALU.add))
                    go(v.tensor_tensor(heads(state[:]), heads(state[:]), per_head(sm[:, 2, :]), ALU.mult))
                    go(v.tensor_tensor(state[:], state[:], ps[6][:], ALU.add), "state_ready")
                else:
                    go(v.tensor_copy(state[:], ps[6][:]), "state_ready")
                k0 = 0 if c else P
                dve.wait_ge(sem("score_ps"), c + 1)
                for b in range(4):
                    src = ps[b][:].rearrange("p (h k) -> p h k", h=2)
                    go(v.scalar_tensor_tensor(prob[:, 2 * b:2 * b + 2, k0:], src[:, :, k0:], float(HD) ** -0.5,
                                              bias[:, 2 * b:2 * b + 2, k0:], ALU.mult, ALU.add), "score_sb")
                go(v.tensor_reduce(sm[:, 10, :], prob[:, :, k0:], AX.X, ALU.max))
                go(v.tensor_tensor(sm[:, 10, :], sm[:, 10, :], hrow[:, 3, :], ALU.max))
                go(v.tensor_tensor(sm[:, 7, :], hrow[:, 3, :], sm[:, 10, :], ALU.subtract))
                go(v.tensor_scalar(sm[:, 6, :], sm[:, 10, :], -1.0, None, ALU.mult), "neg_max")
                if c == NT - 1:
                    dve.wait_ge(sem("early_w_in"), 16)
                    norm_ffn_tile(0, early_w)
                dve.wait_ge(sem("y_ps"), c + 1)
                go(v.tensor_tensor(y1, y1, ps[4][:], ALU.add), "diag_read")
                if c == 0:
                    dve.wait_ge(sem("zv_out"), NT * (LATE + 2 - BY_DVE))
                go(v.tensor_tensor(y1, y1, zs[:, c, :], ALU.mult))
                go(v.tensor_tensor_reduce(y2, y1, y1, 1.0, 0.0, ALU.mult, ALU.add, sm[:, 5, 0:1]))
                rms(sm[:, 5, 1:2], sm[:, 5, 0:1], 512, "dve_step")
                go(v.scalar_tensor_tensor(mix[:, 512:], y1, sm[:, 5, 1:2], wn[:], ALU.mult, ALU.mult), "y_done")
                if c == NT - 1:
                    add_projection(c - 1)
                    dve.wait_ge(sem("s_sb"), 1)
                    search_halves(0)
                    v.drain()
                if 0 < c < NT - 1:
                    add_projection(c - 1)
                dve.wait_ge(sem("prob_exp"), 9 * c + 9)
                go(v.tensor_tensor(sm[:, 11, :], sm[:, 8, :], sm[:, 9, :], ALU.add))
                go(v.reciprocal(sm[:, 11, :], sm[:, 11, :]))
                dve.wait_ge(sem("pv_ps"), c + 1)
                go(v.tensor_tensor(heads(mix[:, 0:512]), heads(ps[2][:]), per_head(sm[:, 11, :]), ALU.mult), "mix_ready")
            def search_sums(r, b):
                v.tensor_tensor(sums.rearrange("p (a b) -> p a b", a=TOPK),
                                pval[:, 0, :].unsqueeze(2).to_broadcast([P, TOPK, TOPK]),
                                pval[:, 1, :].unsqueeze(1).to_broadcast([P, TOPK, TOPK]), ALU.add)
                v.drain()
                top16(sums, tval, tpos)
                v.drain()
                v.tensor_scalar(digit[:, 0, :], tpos, 4, None, ALU.logical_shift_right)
                v.tensor_scalar(digit[:, 1, :], tpos, 15, None, ALU.bitwise_and)
                v.drain()
                v.tensor_copy(digf, digit)
                v.drain()
                v.tensor_tensor(hit, digf.unsqueeze(3).to_broadcast([P, 2, TOPK, TOPK]),
                                iota16.unsqueeze(1).unsqueeze(1).to_broadcast([P, 2, TOPK, TOPK]), ALU.is_equal)
                v.drain()
                v.tensor_tensor(hit, hit, pidf.unsqueeze(2).to_broadcast([P, 2, TOPK, TOPK]), ALU.mult)
                v.drain()
                v.tensor_reduce(part, hit, AX.X, ALU.add)
                v.drain()
                v.scalar_tensor_tensor(pick, part[:, 0, :], float(NK), part[:, 1, :], ALU.mult, ALU.add)
                v.drain()
                v.tensor_copy(idx[:, b, bass.ds(r * TOPK, TOPK)], pick).then_inc(sem("routed"), 1)
                v.tensor_scalar(tdiff, tval, tval[:, 0:1], None, ALU.subtract).then_inc(sem("found"), 1)

            def settle_gates(q, r, b):
                dve.wait_ge(sem("gate_exp"), q + 1)
                v.reciprocal(gsum[:, 1:2], gsum[:, 0:1])
                v.drain()
                v.tensor_scalar(pick, eg, gsum[:, 1:2], None, ALU.mult)
                v.drain()
                v.tensor_copy(gate[:, b, bass.ds(r * TOPK, TOPK)], pick).then_inc(sem("gated"), 1)

            def experts(t, r):
                q = t * PH + r
                late = isinstance(r, int)
                settle = (r + 1, t % 2) if not (late and r + 1 >= PH) else (r + 1 - PH, (t + 1) % 2)
                find = (r + 2, t % 2) if not (late and r + 2 >= PH) else (r + 2 - PH, (t + 1) % 2)
                if t == NT - 1 and late:
                    settle = settle if r + 1 < PH else None
                    find = find if r + 2 < PH else None
                if late and r == PH - 2 and t + 1 < NT:
                    dve.wait_ge(sem("s_sb"), 4 * (t + 2))
                for half in range(2):
                    g = 2 * q + half
                    for i in range(GROUP):
                        dve.wait_ge(sem(f"down{i}"), 16 * g + 16)
                        v.tensor_tensor_reduce(down[:, i, :], down[:, i, :], xn2[:, t % 2, :], 1.0, 0.0,
                                               ALU.mult, ALU.add, pre[:, half, i:i + 1]).then_inc(sem("dots"), 1)
                    dve.wait_ge(sem("gelu"), g + 1)
                    dve.wait_ge(sem("gnow_ready"), g + 1)
                    v.tensor_tensor(actv[:, half], gel[:, half], gnow[:, half], ALU.mult
                                    ).then_inc(sem("act_ready"), 1)
                    if half == 0:
                        if settle:
                            settle_gates(q + 1, *settle)
                        if find:
                            if t == 0 and late and r < 4:
                                dve.wait_ge(sem("s_sb"), r // 2 + 2)
                            search_halves(find[0])
                    elif find:
                        search_sums(*find)

            def finish(t):
                final = xn2[:, t % 2, :]
                acc = ps[4 + 2 * (t % 2)], ps[5 + 2 * (t % 2)]
                dve.wait_ge(sem("fin_sq"), 2 * t + 2)
                go(v.tensor_tensor(ss[:, 14:15], ss[:, 12:13], ss[:, 13:14], ALU.add))
                rms(ss[:, 15:16], ss[:, 14:15], D, "dve_step")
                go(v.scalar_tensor_tensor(final[:, 0:512], acc[0][:], ss[:, 15:16], w_fin[:, 0:512], ALU.mult, ALU.mult))
                go(v.scalar_tensor_tensor(final[:, 512:], acc[1][:], ss[:, 15:16], w_fin[:, 512:], ALU.mult, ALU.mult),
                   "final_ready")

            def prepare(t, part):
                if (t, part) == (1, 0):
                    dve.wait_ge(sem("s_sb"), 4)
                if part == 0 and 0 < t < NT:
                    norm_ffn_tile(t, w_ffn)

            go(v.tensor_copy(iota16, iota16i[:]))
            search_sums(0, 0)
            settle_gates(0, 0, 0)
            search_halves(1)
            v.drain()
            search_sums(1, 0)
            add_projection(NT - 1)
            dve.wait_ge(sem("wffn_in"), 32)
            for t in range(NT):
                tile_steps(dve, t, experts, prepare)
                finish(t)

        @block.tensor
        def _(pe):
            mm = nc.tensor.matmul
            pe.wait_ge(sem("const"), LOADS["const"])
            for t in range(NT):
                pe.wait_ge(sem(f"x_in{t}"), 16)
                for k in range(KT):
                    last = nc.tensor.transpose(ps[2 * t + k // 4][:, (k % 4) * P:(k % 4 + 1) * P],
                                               h[:, t, k * P:(k + 1) * P], ident[:])
                last.then_inc(sem("xT_ps"), 1)
            pe.wait_ge(sem("xT_sb"), 2 * NT)

            def wait_taken(n_step):
                if n_step < BY_DVE:
                    pe.wait_ge(sem("proj_out"), n_step + 1)
                else:
                    pe.wait_ge(sem("zv_out"), NT * (n_step - BY_DVE + 1))

            def project(n_step):
                b = STEPS[n_step]
                bank = ps[step_bank(n_step)]
                if n_step == LATE + 1:
                    wait_taken(LATE)
                elif n_step == LATE + 2:
                    pe.wait_ge(sem("state_ready"), 1)
                elif 4 <= n_step < LATE:
                    wait_taken(n_step - 4)
                if b == DT:
                    pe.wait_ge(sem("wdt_in"), 16)
                    for t in range(NT):
                        for k in range(KT):
                            last = mm(bank[:, t * SH:(t + 1) * SH], xnT[:, k, t * P:(t + 1) * P], w_dt_sb[:, k, :],
                                      start=(k == 0), stop=(k == KT - 1))
                    last.then_inc(sem("step_ps"), 1)
                    return
                pe.wait_ge(sem(f"ring{b % RING}"), 16 * (b // RING + 1))
                w = ring[:, b % RING]
                if b < B_Z:
                    for k in range(KT):
                        last = mm(bank[:], w[:, k, :], xnT[:, k, :], start=(k == 0), stop=(k == KT - 1))
                else:
                    for t in range(NT):
                        for k in range(KT):
                            last = mm(bank[:, t * P:(t + 1) * P], xnT[:, k, t * P:(t + 1) * P], w[:, k, :],
                                      start=(k == 0), stop=(k == KT - 1))
                last.then_inc(sem("step_ps"), 1)
                pe.wait_ge(sem("step_ps"), n_step + 1)
                pe.nop(nofuse=True).then_inc(sem("block_used"), 1)
                if b == 0:
                    pe.wait_ge(sem("r_diag"), NT)
                    mm(ps[5][:], ones[:], r_diag.rearrange("p t c -> p (t c)"), start=True, stop=True
                       ).then_inc(sem("r_ps"), 1)
                    pe.wait_ge(sem("line_in"), 32)
                    pe.wait_ge(sem("rb_ones"), 1)
                    mm(ps[4][0:HEADS, 0:LW], rb[:], buckets, start=True, stop=True).then_inc(sem("line_ps"), 1)

            for n_step in range(LATE):
                project(n_step)
            wait_taken(BY_DVE - 1)
            pe.wait_ge(sem("conv_act"), NXB)
            pe.wait_ge(sem("a_ready"), 1)
            a = dtv[:, 7, :]

            def out_projection(c):
                pe.wait_ge(sem("mixT_sb"), 2 * c + 2)
                pe.wait_ge(sem("wo_in"), 16)
                for b in range(2):
                    if c < NT - 1:
                        pe.wait_ge(sem("state_ready" if b else "off_read"), c + 1 + b)
                    for k in range(KT):
                        last = mm(ps[5 + b][:], mixT[c][:, k, :], wo[:, k, b * 512:(b + 1) * 512], start=(k == 0),
                                  stop=(k == KT - 1))
                last.then_inc(sem("wo_ps"), 1)

            def transpose_normed(t):
                pe.wait_ge(sem("xn2_ready"), t + 1)
                for k in range(KT):
                    last = nc.tensor.transpose(ps[k // 4][:, (k % 4) * P:(k % 4 + 1) * P],
                                               xn2[:, t % 2, k * P:(k + 1) * P], ident[:])
                last.then_inc(sem("xn2T_ps"), 1)

            def queries(t, b):
                if b >= 2:
                    pe.wait_ge(sem("q_sb"), 4 * t + b - 1)
                for j in range(4):
                    for k in range(KT):
                        col = (4 * b + j) * P
                        last = mm(ps[2 + b % 2][:, j * P:(j + 1) * P], wq[:, k, col:col + P], xn2T[:, k, :],
                                  start=(k == 0), stop=(k == KT - 1))
                last.then_inc(sem("q_ps"), 1)

            def scores(t, b, keys=keysT):
                pe.wait_ge(sem("q_sb"), 4 * t + b + 1)
                if b >= 2:
                    pe.wait_ge(sem("s_sb"), 4 * t + b - 1)
                for j in range(4):
                    last = mm(ps[b % 2][:, j * P:(j + 1) * P], qT[:, 4 * b + j, :], keys[:, j % 2, :],
                              start=True, stop=True)
                last.then_inc(sem("s_ps"), 1)

            def chunk_start(c):
                tc = slice(c * P, (c + 1) * P)
                ac = a[:, c * SH:(c + 1) * SH]
                mm(ps[7][:, 0:8], tri[:], ac, start=True, stop=True)
                mm(ps[7][:, 8:16], ones[:], ac, start=True, stop=True).then_inc(sem("acum_ps"), 1)
                for j in range(4):
                    nc.tensor.transpose(ps[0][:, j * P:(j + 1) * P], xconv[:, j, tc], ident[:])
                for g in range(SG):
                    nc.tensor.transpose(ps[1][:, g * P:(g + 1) * P], xconv[:, 4 + g, tc], ident[:])
                for g in range(SG):
                    last = mm(ps[1][:, (2 + g) * P:(3 + g) * P], xconv[:, 4 + g, tc], xconv[:, 6 + g, tc],
                              start=True, stop=True)
                last.then_inc(sem("nat_ps"), 1)

            chunk_start(0)
            for c in range(NT):
                tc = slice(c * P, (c + 1) * P)
                ac = a[:, c * SH:(c + 1) * SH]
                if c == 0:
                    wait_taken(LATE - 1)
                for g in range(SG):
                    bank = ps[2 + g][:].rearrange("p (r l) -> p r l", r=SR)
                    for r in range(SR):
                        hh = g * SR + r
                        last = mm(bank[:, r, :], ac[:, hh:hh + 1].to_broadcast([P, P]), tri[:], start=True, stop=True)
                    last.then_inc(sem("seg_ps"), 1)
                if c == 0:
                    project(LATE)
                if c:
                    pe.wait_ge(sem("mixT_sb"), 2 * c)
                    pe.wait_ge(sem("state_ready"), c)
                    for g in range(SG):
                        mm(ps[5][:, g * 256:(g + 1) * 256], xconv[:, 6 + g, tc], state[:, g * 256:(g + 1) * 256],
                           start=True, stop=True)
                pe.wait_ge(sem("nat_sb"), 2 * c + 2)
                pe.wait_ge(sem("xend"), c + 1)
                for g in range(SG):
                    last = mm(ps[6][:, g * 256:(g + 1) * 256], bnat[:, g * P:(g + 1) * P],
                              xend[:, g * 256:(g + 1) * 256], start=True, stop=True)
                last.then_inc(sem("state_ps"), 1)
                k0 = 0 if c else P
                for hh in range(HEADS):
                    if hh == 4:
                        pe.wait_ge(sem("seg_sb"), SH * (c + 1))
                    half = slice(HD * (hh // 4), HD * (hh // 4) + HD)
                    last = mm(ps[hh // 2][:, (hh % 2) * 256 + k0:(hh % 2) * 256 + 256],
                              qkT[half, 1 + hh % 4, tc], qkT[half, 0, c * P - P + k0:(c + 1) * P], start=True, stop=True)
                last.then_inc(sem("score_ps"), 1)
                pe.wait_ge(sem("lm_ready"), SG * (c + 1))
                for hh in range(SH):
                    last = mm(ps[4][:, hh * SP:(hh + 1) * SP], decay[:, hh // SR, (hh % SR) * P:(hh % SR + 1) * P],
                              xdt[:, hh * SP:(hh + 1) * SP], start=True, stop=True)
                last.then_inc(sem("y_ps"), 1)
                if c == 0:
                    project(LATE + 1)
                    project(LATE + 2)
                else:
                    out_projection(c - 1)
                pe.wait_ge(sem("prob_exp"), 9 * c + 9)
                pe.wait_ge(sem("diag_read"), c + 1)
                if c == NT - 1:
                    transpose_normed(0)
                    pe.wait_ge(sem("wq_in"), 16)
                    pe.wait_ge(sem("early_keys_in"), 32)
                for n_bank, b in enumerate(PT_ORDER[c]):
                    if c == NT - 1 and n_bank == 2:
                        pe.wait_ge(sem("xn2T_sb"), 2)
                        queries(0, 0)
                    for hh in (2 * b, 2 * b + 1):
                        if c == NT - 1 and hh == 4:
                            scores(0, 0, early_keys)
                            pe.wait_ge(sem("s_sb"), 1)
                        for kb in range(0 if c else 1, 2):
                            i = (hh % 2) * 2 + kb
                            last = nc.tensor.transpose(ps[PT[b]][:, i * P:(i + 1) * P],
                                                       prob[:, hh, kb * P:(kb + 1) * P], ident[:])
                    last.then_inc(sem("pt_ps"), 1)
                if c == 0:
                    wait_taken(LATE + 2)
                for n_head, hh in enumerate(2 * b + i for b in PT_ORDER[c] for i in range(2)):
                    pe.wait_ge(sem("pt_sb"), 4 * c + n_head // 2 + 1)
                    for kb in range(0 if c else 1, 2):
                        i = (hh % 2) * 2 + kb
                        last = mm(ps[2][:, hh * HD:(hh + 1) * HD], probT[:, hh // 2, i * P:(i + 1) * P],
                                  v_sb[:, c - 1 + kb, (hh // 4) * HD:(hh // 4 + 1) * HD], start=(kb == 0 or c == 0),
                                  stop=(kb == 1))
                last.then_inc(sem("pv_ps"), 1)
                if c < NT - 1:
                    chunk_start(c + 1)
                pe.wait_ge(sem("mix_ready"), c + 1)
                if c:
                    pe.wait_ge(sem("h_mixed"), c)
                for k in range(KT):
                    last = nc.tensor.transpose(ps[5 + k // 4][:, (k % 4) * P:(k % 4 + 1) * P], mix[:, k * P:(k + 1) * P],
                                               ident[:])
                last.then_inc(sem("mixT_ps"), 1)
            def score_keys(t, part):
                if t == NT:
                    return
                if t == 0:
                    queries(0, 2 + part)
                    scores(0, 2 + part)
                    return
                if (t, part) == (1, 0):
                    pe.wait_ge(sem("s_sb"), 4)
                if part == 0:
                    transpose_normed(t)
                    pe.wait_ge(sem("xn2T_sb"), 2 * t + 2)
                if part < 2:
                    for b in range(2 * part, 2 * part + 2):
                        queries(t, b)
                else:
                    for b in range(4):
                        scores(t, b)

            def experts(t, r):
                acc = ps[4 + 2 * (t % 2)], ps[5 + 2 * (t % 2)]
                for half in range(2):
                    g = t * (SLOTS // GROUP) + 2 * r + half
                    for i in range(GROUP):
                        pe.wait_ge(sem("diag"), 8 * g + i + 1)
                        pe.wait_ge(sem(f"up{i}"), 16 * g + 16)
                        mm(acc[0][:], diag[:, i, :], up[:, i, 0:512], start=False, stop=False, skip_group_check=True)
                        mm(acc[1][:], diag[:, i, :], up[:, i, 512:], start=False, stop=False,
                           skip_group_check=True).then_inc(sem("up_free"), 1)

            out_projection(NT - 1)
            pe.wait_ge(sem("wq_in"), 48)
            queries(0, 1)
            scores(0, 1)
            for t in range(NT):
                if t >= 2:
                    pe.wait_ge(sem("final_ready"), t - 1)
                elif t == 0:
                    pe.wait_ge(sem("h_mixed"), NT)
                for b in range(2):
                    mm(ps[4 + 2 * (t % 2) + b][:], ident[:], h[:, t, b * 512:(b + 1) * 512], start=True, stop=False,
                       skip_group_check=True)
                tile_steps(pe, t, experts, score_keys)
                pe.wait_ge(sem("up_free"), 8 + SLOTS * (t + 1))
                pe.nop(nofuse=True).then_inc(sem("peer_done"), 1)


def bucket_lines():
    dist = P + P - 1 - np.arange(LW)
    n = np.maximum(dist, 0)
    exact = N_BUCKETS // 2
    nf = np.maximum(n, 1).astype(np.float32)
    large = exact + (np.log(nf / np.float32(exact)) / np.float32(math.log(MAX_DISTANCE / exact))
                     * np.float32(N_BUCKETS - exact)).astype(np.int32)
    large = np.minimum(large, N_BUCKETS - 1)
    which = np.where(n < exact, n, large)
    ok = (dist >= 0) & (dist < WINDOW)
    lines = np.zeros((N_BUCKETS + 1, LW), np.float32)
    lines[which[ok], np.nonzero(ok)[0]] = 1.0
    lines[N_BUCKETS, ~ok] = NEG
    return lines


def kernel(**inputs):
    import numpy as _np
    import concourse.bacc as _bacc
    from concourse import mybir as _mybir
    from concourse.bass_utils import run_bass_kernel_spmd as _run

    g = {k: _np.asarray(a) for k, a in inputs.items()}
    w = g["w_in"][0]
    kv = HEADS * HD
    off_v, off_z = kv + KV_HEADS * HD, kv + 2 * KV_HEADS * HD
    off_x = off_z + SH * SP
    off_dt = off_x + XBC
    cols = [_np.arange(off_x + j * P, off_x + (j + 1) * P) for j in range(NXB)]
    cols += [_np.arange(kv, off_v)]
    cols += [_np.concatenate([_np.arange(j * HD, (j + 1) * HD), _np.arange((4 + j) * HD, (5 + j) * HD)]) for j in range(4)]
    cols += [_np.arange(off_z + j * P, off_z + (j + 1) * P) for j in range(4)]
    cols += [_np.arange(off_v, off_z)]

    def by_rows(m):
        return _np.ascontiguousarray(m.reshape(KT, P, m.shape[1]).transpose(1, 0, 2).reshape(P, -1))

    host = {
        "x": g["x"], "w_in_blocks": _np.stack([by_rows(w[:, c]) for c in cols]), "w_dt": by_rows(w[:, off_dt:]),
        "norm_mix": g["norm_mix"][0].reshape(KT, P).T,
        "conv_w": g["conv_w"][0].reshape(CONV, NXB, P).transpose(2, 0, 1), "conv_b": g["conv_b"][0].reshape(NXB, P).T,
        "dt_bias": g["dt_bias"],
        "a_log": g["a_log"], "d_skip": g["d_skip"], "ssd_norm_w": g["ssd_norm_w"], "sinks": g["attn_sinks"],
        "w_out": g["w_out"][0], "rel_bias": g["rel_bias"], "bucket_line": bucket_lines(), "norm_ffn": g["norm_ffn"],
        "w_query": g["w_query"][0], "keys1_t": g["sub_keys1"][0].T, "keys2_t": g["sub_keys2"][0].T,
        "expert_down": g["expert_down"][0], "expert_up": g["expert_up"][0], "norm_final": g["norm_final"][None],
    }
    nc = _bacc.Bacc("TRN2", target_bir_lowering=False, num_devices=1)
    arrays, args = {}, []
    for name, a in host.items():
        a = _np.ascontiguousarray(a)
        arrays[f"in_{name}_dram"] = a
        args.append(nc.dram_tensor(f"in_{name}_dram", a.shape, _mybir.dt.from_np(a.dtype), kind="ExternalInput").ap())
    out = nc.dram_tensor("out_0_dram", (1, SEQ, D), F32, kind="ExternalOutput").ap()
    layer(nc, *args, out)
    r = _run(nc, [arrays], core_ids=[0])
    return r.results[0]["out_0_dram"]
```
